# Optimizing a Trainium2 kernel written in Bass

```python
import math
import jax, jax.numpy as jnp
from jax import lax
import numpy as np

D_MODEL = 1024
BATCH = 1
SEQ = 512
DEPTH = 1

CHUNK = 64
Q_BLOCK = 128
ROPE_THETA = 500000.0
NORM_EPS = 1e-6

A_HEADS = 8
A_HEAD_DIM = 64
IDX_HEADS = 8
IDX_DIM = 64
TOPK_KEYS = 256
B_HEADS = 4
B_QK_DIM = 64
B_V_DIM = 2 * B_QK_DIM
ROT_DIM = A_HEAD_DIM // 4
N_EXPERTS = 32
TOP_EXPERTS = 4
D_EXPERT = 1024
SWIGLU_LIMIT = 7.0
SWIGLU_ALPHA = 1.702
MOE_BLOCK = 128

SPLITS = (A_HEADS * A_HEAD_DIM,
          A_HEAD_DIM,
          A_HEAD_DIM,
          IDX_HEADS * IDX_DIM,
          IDX_DIM,
          IDX_HEADS,
          B_HEADS * 2 * B_QK_DIM,
          B_HEADS * 2 * B_QK_DIM,
          B_HEADS * B_V_DIM)
D_IN = sum(SPLITS)
SPLIT_OFFSETS = np.cumsum(SPLITS)[:-1].tolist()
D_MIX = A_HEADS * A_HEAD_DIM + B_HEADS * B_V_DIM

kernel_name = 'hybrid_dsa_diffattn_moe_block'

def rms_norm(x, g):
    x32 = x.astype(jnp.float32)
    y = x32 * lax.rsqrt(jnp.mean(x32 * x32, axis=-1, keepdims=True) + NORM_EPS)
    return (y * g.astype(jnp.float32)).astype(x.dtype)

def rope_tables(positions):
    inv_freq = ROPE_THETA ** (-jnp.arange(0, ROT_DIM, 2, dtype=jnp.float32) / ROT_DIM)
    ang = positions.astype(jnp.float32)[..., None] * inv_freq
    return jnp.cos(ang), jnp.sin(ang)

def partial_rope(x, cos, sin):
    half = ROT_DIM // 2
    c = cos[:, :, None, :]
    s = sin[:, :, None, :]
    x1 = x[..., :half].astype(jnp.float32)
    x2 = x[..., half:ROT_DIM].astype(jnp.float32)
    rot = jnp.concatenate([x1 * c - x2 * s, x2 * c + x1 * s], axis=-1).astype(x.dtype)
    return jnp.concatenate([rot, x[..., ROT_DIM:]], axis=-1)

def to_blocks(t):
    b, s = t.shape[:2]
    return jnp.moveaxis(t.reshape(b, s // Q_BLOCK, Q_BLOCK, *t.shape[2:]), 1, 0)

def from_blocks(t):
    nb, b, qb = t.shape[:3]
    return jnp.moveaxis(t, 0, 1).reshape(b, nb * qb, *t.shape[3:])

def dsa_mixer(q, k, v, qi, ki, wi, k_sel):
    s_len = q.shape[1]
    key_chunk = jnp.arange(s_len) // CHUNK
    kv = jnp.concatenate([k, v], axis=-1)

    def block(args):
        bi, qb, qib, wib = args
        q_chunk = (bi * Q_BLOCK + jnp.arange(Q_BLOCK)) // CHUNK
        admissible = key_chunk[None, :] <= q_chunk[:, None]
        rel = jax.nn.relu(jnp.einsum('bqhd,bsd->bqhs', qib, ki).astype(jnp.float32))
        score = jnp.einsum('bqhs,bqh->bqs', rel, wib.astype(jnp.float32))
        score = jnp.where(admissible[None], score, -jnp.inf)
        _, idx = lax.top_k(score, k_sel)
        valid = key_chunk[idx] <= q_chunk[None, :, None]
        kv_sel = jax.vmap(lambda kvb, ib: kvb[ib])(kv, idx)
        k_sel_, v_sel = kv_sel[..., :A_HEAD_DIM], kv_sel[..., A_HEAD_DIM:]
        logits = jnp.einsum('bqhd,bqkd->bqhk', qb, k_sel_).astype(jnp.float32) * (A_HEAD_DIM ** -0.5)
        logits = jnp.where(valid[:, :, None, :], logits, -jnp.inf)
        p = jax.nn.softmax(logits, axis=-1).astype(v.dtype)
        return jnp.einsum('bqhk,bqkd->bqhd', p, v_sel)

    nb = s_len // Q_BLOCK
    out = lax.map(block, (jnp.arange(nb), to_blocks(q), to_blocks(qi), to_blocks(wi)))
    return from_blocks(out)

def diff_mixer(q1, q2, k1, k2, v, lam, lam_init, g_subln):
    s_len = q1.shape[1]
    key_chunk = jnp.arange(s_len) // CHUNK
    scale = B_QK_DIM ** -0.5

    def block(args):
        bi, q1b, q2b = args
        q_chunk = (bi * Q_BLOCK + jnp.arange(Q_BLOCK)) // CHUNK
        mask = (key_chunk[None, :] <= q_chunk[:, None])[None, None]
        s1 = jnp.einsum('bqhd,bshd->bhqs', q1b, k1).astype(jnp.float32) * scale
        s2 = jnp.einsum('bqhd,bshd->bhqs', q2b, k2).astype(jnp.float32) * scale
        p1 = jax.nn.softmax(jnp.where(mask, s1, -jnp.inf), axis=-1)
        p2 = jax.nn.softmax(jnp.where(mask, s2, -jnp.inf), axis=-1)
        a = (p1 - lam * p2).astype(v.dtype)
        return jnp.einsum('bhqs,bshd->bqhd', a, v)

    nb = s_len // Q_BLOCK
    o = from_blocks(lax.map(block, (jnp.arange(nb), to_blocks(q1), to_blocks(q2))))
    return rms_norm(o, g_subln) * (1.0 - lam_init)

def moe(h, w_router, b_router, w_gu, b_gu, w_down, b_down):
    b, s, d = h.shape
    n = b * s
    hf = h.reshape(n, d)
    logits = (hf @ w_router + b_router).astype(jnp.float32)
    top_vals, top_idx = lax.top_k(logits, TOP_EXPERTS)
    gates = jax.nn.softmax(top_vals, axis=-1)

    nk = n * TOP_EXPERTS
    flat_e = top_idx.reshape(-1)
    flat_tok = jnp.repeat(jnp.arange(n, dtype=jnp.int32), TOP_EXPERTS)
    flat_g = gates.reshape(-1)
    order = jnp.argsort(flat_e)
    e_sorted = flat_e[order]
    tok_sorted = flat_tok[order]
    g_sorted = flat_g[order]
    counts = jnp.bincount(flat_e, length=N_EXPERTS)
    padded = ((counts + MOE_BLOCK - 1) // MOE_BLOCK) * MOE_BLOCK
    start = jnp.cumsum(counts) - counts
    pend = jnp.cumsum(padded)
    pstart = pend - padded
    dest = pstart[e_sorted] + (jnp.arange(nk) - start[e_sorted])
    n_blocks = -(-(nk + N_EXPERTS * (MOE_BLOCK - 1)) // MOE_BLOCK)
    m = n_blocks * MOE_BLOCK
    slot_tok = jnp.full((m,), n, dtype=jnp.int32).at[dest].set(tok_sorted)
    slot_g = jnp.zeros((m,), jnp.float32).at[dest].set(g_sorted)
    block_expert = jnp.minimum(
        jnp.searchsorted(pend, jnp.arange(n_blocks) * MOE_BLOCK, side='right'), N_EXPERTS - 1)
    h_pad = jnp.concatenate([hf, jnp.zeros((1, d), hf.dtype)], axis=0)

    def expert_block(args):
        tok, g, e = args
        xb = h_pad[tok]
        gu = xb @ w_gu[e] + b_gu[e]
        glu = jnp.minimum(gu[:, :D_EXPERT], SWIGLU_LIMIT)
        lin = jnp.clip(gu[:, D_EXPERT:], -SWIGLU_LIMIT, SWIGLU_LIMIT)
        act = glu * jax.nn.sigmoid(SWIGLU_ALPHA * glu) * (lin + 1.0)
        return (act @ w_down[e] + b_down[e]) * g[:, None].astype(h.dtype)

    ys = lax.map(expert_block, (slot_tok.reshape(n_blocks, MOE_BLOCK),
                                slot_g.reshape(n_blocks, MOE_BLOCK), block_expert))
    out = jax.ops.segment_sum(ys.reshape(m, d), slot_tok, num_segments=n + 1)[:n]
    return out.reshape(b, s, d).astype(h.dtype)

def setup_inputs(seed: int = 0) -> dict:
    key = jax.random.key(seed)
    ks = jax.random.split(key, 24)
    f32 = jnp.float32
    L = DEPTH
    nrm = lambda k, shape, scale: jax.random.normal(k, shape, f32) * scale
    gain = lambda k, shape: 1.0 + 0.02 * jax.random.normal(k, shape, f32)
    x = jax.random.normal(ks[0], (BATCH, SEQ, D_MODEL), f32)
    offsets = jax.random.randint(ks[1], (BATCH, 1), 0, 4096) * CHUNK
    positions = (offsets + jnp.arange(SEQ)[None, :]).astype(jnp.int32)
    return {
        'x': x,
        'positions': positions,
        'g_attn': gain(ks[2], (L, D_MODEL)),
        'w_in': nrm(ks[3], (L, D_MODEL, D_IN), D_MODEL ** -0.5),
        'g_qa': gain(ks[4], (L, A_HEAD_DIM)),
        'g_ka': gain(ks[5], (L, A_HEAD_DIM)),
        'g_idx_k': gain(ks[6], (L, IDX_DIM)),
        'lambda_q1': nrm(ks[7], (L, B_QK_DIM), 0.1),
        'lambda_k1': nrm(ks[8], (L, B_QK_DIM), 0.1),
        'lambda_q2': nrm(ks[9], (L, B_QK_DIM), 0.1),
        'lambda_k2': nrm(ks[10], (L, B_QK_DIM), 0.1),
        'g_qb': gain(ks[11], (L, B_QK_DIM)),
        'g_kb': gain(ks[12], (L, B_QK_DIM)),
        'g_subln': gain(ks[13], (L, B_V_DIM)),
        'w_o': nrm(ks[14], (L, D_MIX, D_MODEL), D_MIX ** -0.5),
        'g_ffn': gain(ks[15], (L, D_MODEL)),
        'w_router': nrm(ks[16], (L, D_MODEL, N_EXPERTS), D_MODEL ** -0.5),
        'b_router': nrm(ks[17], (L, N_EXPERTS), 0.01),
        'w_gu': nrm(ks[18], (L, N_EXPERTS, D_MODEL, 2 * D_EXPERT), D_MODEL ** -0.5),
        'b_gu': nrm(ks[19], (L, N_EXPERTS, 2 * D_EXPERT), 0.02),
        'w_down': nrm(ks[20], (L, N_EXPERTS, D_EXPERT, D_MODEL), D_EXPERT ** -0.5),
        'b_down': nrm(ks[21], (L, N_EXPERTS, D_MODEL), 0.02),
    }

def reference(x, positions, g_attn, w_in, g_qa, g_ka, g_idx_k, lambda_q1, lambda_k1,
              lambda_q2, lambda_k2, g_qb, g_kb, g_subln, w_o, g_ffn, w_router, b_router,
              w_gu, b_gu, w_down, b_down):
    b, s, _ = x.shape
    k_sel = min(TOPK_KEYS, s // 4)
    cos, sin = rope_tables(positions)
    for layer in range(DEPTH):
        lam_init = 0.8 - 0.6 * math.exp(-0.3 * layer)
        h = rms_norm(x, g_attn[layer])
        proj = h @ w_in[layer]
        aq, ak, av, iq, ik, iw, bq, bk, bv = jnp.split(proj, SPLIT_OFFSETS, axis=-1)

        aq = partial_rope(rms_norm(aq.reshape(b, s, A_HEADS, A_HEAD_DIM), g_qa[layer]), cos, sin)
        ak = partial_rope(rms_norm(ak, g_ka[layer])[:, :, None], cos, sin)[:, :, 0]
        iq = partial_rope(iq.reshape(b, s, IDX_HEADS, IDX_DIM), cos, sin)
        ik = partial_rope(rms_norm(ik, g_idx_k[layer])[:, :, None], cos, sin)[:, :, 0]
        iw = iw * ((IDX_HEADS * IDX_DIM) ** -0.5)
        y_a = dsa_mixer(aq, ak, av, iq, ik, iw, k_sel).reshape(b, s, A_HEADS * A_HEAD_DIM)

        bq = bq.reshape(b, s, B_HEADS, 2, B_QK_DIM)
        bk = bk.reshape(b, s, B_HEADS, 2, B_QK_DIM)
        q1 = partial_rope(rms_norm(bq[:, :, :, 0], g_qb[layer]), cos, sin)
        q2 = partial_rope(rms_norm(bq[:, :, :, 1], g_qb[layer]), cos, sin)
        k1 = partial_rope(rms_norm(bk[:, :, :, 0], g_kb[layer]), cos, sin)
        k2 = partial_rope(rms_norm(bk[:, :, :, 1], g_kb[layer]), cos, sin)
        bv = bv.reshape(b, s, B_HEADS, B_V_DIM)
        lam = (jnp.exp(jnp.sum(lambda_q1[layer].astype(jnp.float32) * lambda_k1[layer].astype(jnp.float32)))
               - jnp.exp(jnp.sum(lambda_q2[layer].astype(jnp.float32) * lambda_k2[layer].astype(jnp.float32)))
               + lam_init)
        y_b = diff_mixer(q1, q2, k1, k2, bv, lam, lam_init, g_subln[layer]).reshape(b, s, B_HEADS * B_V_DIM)

        x = x + jnp.concatenate([y_a, y_b], axis=-1) @ w_o[layer]
        x = x + moe(rms_norm(x, g_ffn[layer]), w_router[layer], b_router[layer],
                    w_gu[layer], b_gu[layer], w_down[layer], b_down[layer])
    return x


_drawn_inputs = setup_inputs


def setup_inputs(seed=0):
    import zlib

    import numpy as np

    out = dict(_drawn_inputs(seed))
    spreads = {}
    factors = {'g_qa': 4.275,
     'g_ka': 6.712,
     'lambda_k2': 12.84,
     'b_gu': 5.723,
     'b_down': 6.583,
     'b_router': 3.193,
     'g_kb': 2.79}
    for name, (base, spread) in spreads.items():
        noise = np.random.default_rng([zlib.crc32(name.encode()), seed]).standard_normal(out[name].shape)
        drawn = base * np.exp(spread * noise) if base else spread * noise
        out[name] = __import__('jax').numpy.asarray(drawn.astype(out[name].dtype))
    for name, factor in factors.items():
        out[name] = (out[name] * factor).astype(out[name].dtype)
    return out
```

```python
import math
from contextlib import ExitStack

import numpy as np

import concourse.bass as bass
from concourse import mybir

ALU = mybir.AluOpType
ACT = mybir.ActivationFunctionType
AX = mybir.AxisListType
F32 = mybir.dt.float32
F32R = mybir.dt.float32r
BF16 = mybir.dt.bfloat16
I32 = mybir.dt.int32
U32 = mybir.dt.uint32

P = 128
SEQ, D = 512, 1024
T = SEQ // P
KD = D // P
CHUNK = 64
ROPE_THETA = 500000.0
EPS = 1e-6
HA, HI, HB, HD = 8, 8, 4, 64
ROT = HD // 4
HALF = ROT // 2
TOPK = min(256, SEQ // 4)
E, TOPE, DE = 32, 4, 1024
LIMIT, ALPHA = 7.0, 1.702
LAM_INIT = 0.8 - 0.6 * math.exp(0.0)
FAR = 2 ** 14
INV_FREQ = np.array([ROPE_THETA ** (-j / ROT) for j in range(0, ROT, 2)]).astype(np.float32)
ROUND_BY = 1.5 * 2.0 ** 23
TWO_PI = (201 / 32, 253 / 128 * 2.0 ** -10, 2 * math.pi - 201 / 32 - 253 / 128 * 2.0 ** -10)
PI_BELOW = 3.1415925
MASKED = -1e30
TAKEN = -3e38

O_AQ, O_AK, O_AV, O_IQ = 0, 512, 576, 640
O_IK, O_IW, O_BQ, O_BK, O_BV = 1152, 1216, 1224, 1736, 2248
CHUNKS = [("iq", [(O_IQ, 512)]), ("kvi", [(O_IK, 72), (O_AK, 128)]), ("aq", [(O_AQ, 512)]),
          ("bv", [(O_BV, 512)]), ("bq", [(O_BQ, 512)]), ("bk", [(O_BK, 512)])]
C_IW, C_AV = 64, 136
WO = len(CHUNKS)
WIDTH = [sum(n for _, n in c[1]) for c in CHUNKS] + [512, 512]

ITEMS = [(c, t) for c in range(len(CHUNKS)) for t in range(T) if not (CHUNKS[c][0] == "iq" and t == 0)]
ITEM_NO = {it: u for u, it in enumerate(ITEMS)}
ROUNDS_TOPK = TOPK // 8


def has_heads(u):
    return CHUNKS[ITEMS[u][0]][0] != "bv"


def keys_of(t):
    return P * (t + 1)


def make_plan():
    plan = [("turn_h", k) for k in range(KD)]
    pieces = [("split_w", m) for m in range(4 * (WO + 2))]
    plan += pieces[0:4]
    del pieces[0:4]
    scores = [("iscore", t, h) for t in range(1, T) for h in range(HI)]
    search = [("topk", t, r) for t in range(1, T) for r in range(ROUNDS_TOPK)]

    def next_search(n):
        for _ in range(n):
            if search and ("iscore", search[0][1], HI - 1) in plan:
                plan.append(search.pop(0))

    n_items = len(ITEMS)
    for s in range(n_items + 3):
        norm = 0 <= s - 2 < n_items and has_heads(s - 2)
        if norm:
            plan.append(("norm", s - 2))
        if s < n_items:
            while pieces and pieces[0][1] <= 4 * ITEMS[s][0] + 4 + ITEMS[s][1] and pieces[0][1] < 4 * WO:
                plan.append(pieces.pop(0))
        if 0 <= s - 1 < n_items and has_heads(s - 1):
            plan.append(("sums", s - 1))
        if norm:
            plan.append(("rope", s - 2))
        if 0 <= s - 3 < n_items and has_heads(s - 3):
            plan.append(("turn_heads", s - 3))
        if norm:
            plan.append(("split_heads", s - 2))
        if s < n_items:
            plan.append(("proj", s))
        if s >= 10:
            for _ in range(3):
                if scores:
                    plan.append(scores.pop(0))
            next_search(3)
    plan += pieces

    units = [(t, j) for t in range(T) for j in range(16)]

    def product_of(n):
        if not 0 <= n < len(units):
            return None
        t, j = units[n]
        if j < 8:
            return ("B", t, j // 2) if j % 2 else None
        return ("A", t, j - 8)

    late = {2: ["mix"], 4: ["mix_norm"], 5: ["turn_y"], 14: ["post"], 15: ["post_mean"],
            16: ["post_norm"], 17: ["turn_h2"], 18: ["route"]}
    for n in range(len(units) + 19):
        if n < len(units):
            t, j = units[n]
            if t >= 1 and j == 7:
                while search and search[0][1] <= t:
                    plan.append(search.pop(0))
                plan.append(("mask", t))
            plan.append(("score", n))
            next_search(1)
        if product_of(n - 1):
            plan.append(("turn_p", product_of(n - 1)))
        if product_of(n - 2):
            plan.append(("values", product_of(n - 2)))
        for t in range(T):
            lag = n - 16 * (t + 1)
            if 6 <= lag < 6 + KD:
                plan.append(("out_proj", t, lag - 6))
            for kind in late.get(lag, []):
                plan.append((kind, t))
    return plan


PLAN = make_plan()


def number(kinds, count=lambda st: 1):
    at, out = 0, {}
    for st in PLAN:
        if st[0] in kinds:
            out[st] = at
            at += count(st)
    out["all"] = at
    return out


def turns_in(st):
    if st[0] == "turn_heads":
        name = CHUNKS[ITEMS[st[1]][0]][0]
        return {"iq": 2, "aq": 2, "bq": 2, "kvi": 1, "bk": 4}[name]
    return {"turn_h": 1, "turn_p": 1, "turn_y": 2, "turn_h2": 2}[st[0]]


TURN = number(("turn_h", "turn_heads", "turn_p", "turn_y", "turn_h2"), turns_in)
SPLIT = number(("turn_h", "turn_y"), turns_in)
SCORE = number(("iscore", "score"))
PROD = number(("turn_p",))
HEADED = [u for u in range(len(ITEMS)) if has_heads(u)]
NORMED = [u for u in HEADED if CHUNKS[ITEMS[u][0]][0] != "iq"]
N_TOPK_SCORES = HI * (T - 1)

NG, ND = KD, KD // 2
NCH = NG + ND
RAW, HL = 6, 4
ROUNDS = SEQ // P


def build(nc, x, positions, g_attn, w_in, g_qa, g_ka, g_idx_k, lambda_q1, lambda_k1,
          lambda_q2, lambda_k2, g_qb, g_kb, g_subln, w_o, g_ffn, w_router, b_router,
          w_gu, b_gu, w_down, b_down, out, dbg=None):
    with ExitStack() as ctx:
        at = {"free": 16512}

        def place(name, shape, dt, offset=None):
            size = int(np.prod(shape[1:])) * mybir.dt.size(dt)
            size = -(-size // 32) * 32
            if offset is None:
                offset = at["free"]
                at["free"] += size
            t = nc.alloc_sbuf_tensor_at(name, shape, dt, offset=offset)
            return t.ap() if hasattr(t, "ap") else t

        def sem(name):
            return ctx.enter_context(nc.semaphore(name))

        base = at["free"]
        W0 = place("W0", [P, 2, KD, 512], F32R)
        QA = place("QA", [P, HA, SEQ], F32R)
        W1 = place("W1", [P, 2, KD, 512], F32R)
        HT = place("HT", [P, 2, KD, SEQ], F32R)
        QB = place("QB", [P, 2 * HB, SEQ], F32R)
        KAI = place("KAI", [P, 2, 2, SEQ], F32R)
        stk = place("stk", [P, 2, 8, P], F32R)
        WR = place("WR", [P, 4, 1024], F32)
        VB = place("VB", [P, T, 512], F32)
        VA = place("VA", [P, T, HD], F32)
        raw = place("raw", [P, 4, 512], F32)
        sq = place("sq", [P, 2, 512], F32)
        work = place("work", [P, T - 1, SEQ], F32)
        rel = place("rel", [P, 2, SEQ], F32)
        maskA = place("maskA", [P, T, SEQ], BF16)
        kept = at["free"]
        xs = place("xs", [P, T, D], F32, offset=base + 32768)
        squares = place("squares", [P, T, D], F32, offset=base + 49152)
        KB = W0
        IQ = QB
        Ew = raw
        PT = sq
        y = WR[:, 0, :]
        xres = WR[:, 1, :]
        h2 = WR[:, 2, :]
        x1 = WR[:, 3, :]
        yT = stk
        h2T = xres.rearrange("p (k n) -> p k n", k=KD)
        GF = rel.rearrange("p a b -> p (a b)")
        wraw = place("wraw", [P, RAW, 2048], F32, offset=base)
        whl = place("whl", [P, HL, 2, 2048], F32R, offset=base + 49152)
        o_qb = base + 49152 + 65536
        xbase = place("xbase", [P, T, D], F32, offset=o_qb)
        aT = place("aT", [P, 2, KD, P], F32R, offset=o_qb + 16384)
        xT = place("xT", [P, 2, KD, P], F32R, offset=o_qb + 24576)
        acts = place("acts", [P, 4, 1024], F32, offset=o_qb + 32768)
        bgs = place("bgs", [64, 2048], F32R, offset=o_qb + 49152)
        oh = place("oh", [P, T, P], BF16, offset=o_qb + 57344)
        ysb = place("ysb", [P, D], F32, offset=o_qb + 57344 + 1024)
        xg = place("xg", [P, D], F32, offset=o_qb + 57344 + 1024 + 8192)
        yk = place("yk", [P, 2, TOPE, D], F32, offset=base)
        bdn = place("bdn", [E, D], F32, offset=o_qb + 57344 + 1024 + 4096)
        bg_raw = acts[0:64, 0:2, :].rearrange("p a n -> p (a n)")
        o_work = o_qb + 57344 + 1024 + 8192 + 4096
        one = place("one", [P, T, TOPE, E], F32, offset=o_work)
        onek = place("onek", [P, T, TOPE, E], F32, offset=o_work + 2048)
        gden = place("gden", [P, T, E], F32, offset=o_work + 4096)
        gdT = place("gdT", [E, SEQ], F32, offset=o_work + 4608)
        kef = place("kef", [P, T, E], F32, offset=o_work + 6656)
        at["free"] = kept
        ident = place("ident", [P, P], F32)
        identb = place("identb", [P, P], BF16)
        causal = place("causal", [P, P], BF16)
        gcol = place("gcol", [P, KD], F32)
        gh = place("gh", [P, 5, HD], F32)
        gsub = place("gsub", [P, 2 * HD], F32)
        posi = place("posi", [P, T], I32)
        posf = place("posf", [P, T], F32)
        ang = place("ang", [P, T, HALF], F32)
        cyc = place("cyc", [P, T, HALF], F32)
        cosr = place("cosr", [P, T, ROT], F32)
        sinr = place("sinr", [P, T, ROT], F32)
        lamv = place("lamv", [P, 4, HD], F32)
        lams = place("lams", [P, 8], F32)
        half = place("half", [P, 16], F32)
        ss = place("ss", [P, 5, 8], F32)
        rstd = place("rstd", [P, 5, 8], F32)
        rp = place("rp", [P, 2, 8, ROT], F32)
        iw = place("iw", [P, T, HI], F32)
        top = place("top", [P, 8], F32)
        nmax = place("nmax", [P, 2, 16], F32)
        lsum = place("lsum", [P, 2, 16], F32)
        ratio = place("ratio", [P, 2, HB], F32)
        rl = place("rl", [P, 16], F32)
        tss = place("tss", [P, 4], F32)
        wrt = place("wrt", [P, KD, E], F32)
        brt = place("brt", [P, E], F32)
        lg = place("lg", [P, T, E], F32)
        top8 = place("top8", [P, T, 8], F32)
        idx8 = place("idx8", [P, T, 8], U32)
        idxf = place("idxf", [P, T, TOPE], F32)
        gate = place("gate", [P, T, TOPE], F32)
        gsum = place("gsum", [P, T], F32)
        iota = place("iota", [P, P], F32)
        tri = place("tri", [P, P], BF16)
        ones = place("ones", [P, P], BF16)
        selm = place("selm", [P, T, E], F32)
        selb = place("selb", [P, T, E], BF16)
        rank = place("rank", [P, T, E + 1], F32)
        ke = place("ke", [P, T, E + 1], BF16)
        r1f = place("r1f", [P, 2], F32)
        r1 = place("r1", [P, 2], BF16)
        r2 = place("r2", [P, T, 2], BF16)
        off = place("off", [P, 2], F32)
        idx2 = place("idx2", [P, 2], U32)
        rows = place("rows", [P, 3], U32)
        zero = place("zero", [P, 1], U32)
        passed = place("passed", [P, 3], U32)
        cmax = place("cmax", [P, 1], F32)
        cnt = place("cnt", [P, 1], I32)
        pick = place("pick", [64, E + 1], F32)
        sel = place("sel", [64, P], F32R)
        assert at["free"] <= nc.sbuf_usable_end, at["free"]

        ps = ctx.enter_context(nc.psum_tensor("ps", [P, 8, 512], F32))
        S_BANK, TP_BANK, ACC, OB, OA = 0, 2, 4, 6, 7
        GU, DN, TP = 0, 4, 6

        hd = nc.dram_tensor("h_rows", (SEQ, D), F32).ap()
        x1d = nc.dram_tensor("x1_rows", (SEQ, D), F32).ap()
        yd = nc.dram_tensor("expert_rows", (SEQ * TOPE, D), F32).ap()

        x_in = [sem(f"x_in{t}") for t in range(T)]
        small_in = sem("small_in")
        piece_in = [sem(f"piece_in{s}") for s in range(4)]
        xres_in = sem("xres_in")
        gf_in = sem("gf_in")
        const = sem("const")
        pool_step = sem("pool_step")
        dve_step = sem("dve_step")
        x_sum = sem("x_sum")
        x_mean = sem("x_mean")
        x_root = sem("x_root")
        h_ok = sem("h_ok")
        angles = sem("angles")
        sines = sem("sines")
        lam_in = sem("lam_in")
        lam_exp = sem("lam_exp")
        turned = sem("turned")
        turn_read = [sem("turn_read0"), sem("turn_read1")]
        hi_ok = sem("hi_ok")
        w_hi = sem("w_hi")
        w_lo = sem("w_lo")
        projected = sem("projected")
        raw_ok = sem("raw_ok")
        squared = sem("squared")
        summed = sem("summed")
        rooted = sem("rooted")
        scaled = sem("scaled")
        gained = sem("gained")
        roped = sem("roped")
        heads_hi = sem("heads_hi")
        heads_lo = sem("heads_lo")
        score_ps = sem("score_ps")
        score_read = sem("score_read")
        rel_used = sem("rel_used")
        mask_ok = sem("mask_ok")
        max_ok = sem("max_ok")
        combined = sem("combined")
        values_ok = sem("values_ok")
        o_read = sem("o_read")
        yss = sem("yss")
        yroot = sem("yroot")
        y_ok = sem("y_ok")
        acc_ps = sem("acc_ps")
        x1_ok = sem("x1_ok")
        x1_sq = sem("x1_sq")
        x1_mean = sem("x1_mean")
        x1_root = sem("x1_root")
        h2_ok = sem("h2_ok")
        logit_ps = sem("logit_ps")
        logit_ok = sem("logit_ok")
        rows_out = sem("rows_out")
        gates_in = sem("gates_in")
        gates_exp = sem("gates_exp")
        picked = sem("picked")
        gden_ok = sem("gden_ok")
        gd_ps = sem("gd_ps")
        gd_ok = sem("gd_ok")
        rank_ps = sem("rank_ps")
        routed = sem("routed")
        xbase_in = sem("xbase_in")
        bg_in = sem("bg_in")
        bg_hi = sem("bg_hi")
        bg_ok = sem("bg_ok")
        bterm_ps = sem("bterm_ps")
        base_ok = sem("base_ok")
        landed = [sem(f"landed{s}") for s in range(RAW)]
        chunk_hi = sem("chunk_hi")
        chunk_lo = sem("chunk_lo")
        chunk_used = sem("chunk_used")
        slots_ok = sem("slots_ok")
        pick_ok = sem("pick_ok")
        idx_ps = sem("idx_ps")
        idx_ok = sem("idx_ok")
        row_ok = sem("row_ok")
        xg_clear = sem("xg_clear")
        gathered = sem("gathered")
        xT_ps = sem("xT_ps")
        xT_hi = sem("xT_hi")
        xT_lo = sem("xT_lo")
        bias_mm = sem("bias_mm")
        glu_ok = sem("glu_ok")
        sig_ok = sem("sig_ok")
        lin_ok = sem("lin_ok")
        prod_ok = sem("prod_ok")
        act_ok = sem("act_ok")
        aT_ps = sem("aT_ps")
        aT_hi = sem("aT_hi")
        aT_lo = sem("aT_lo")
        yrow_ok = sem("yrow_ok")
        scattered = sem("scattered")
        round_step = sem("round_step")
        experts_done = sem("experts_done")
        yk_in = [sem("yk_in0"), sem("yk_in1")]
        out_ok = sem("out_ok")
        stored = sem("stored")

        def rows_of(t):
            return slice(t * P, (t + 1) * P)

        def bc(row):
            return row[0].partition_broadcast(P)

        small = [
            (posi, positions[0].rearrange("(t p) -> p t", p=P)),
            (gcol, g_attn[0].rearrange("(k p) -> p k", p=P)),
            (gh[:, 0, :], bc(g_qa)), (gh[:, 1, :], bc(g_qb)), (gh[:, 2, :], bc(g_kb)),
            (gh[:, 3, :], bc(g_idx_k)), (gh[:, 4, :], bc(g_ka)),
            (lamv[:, 0, :], bc(lambda_q1)), (lamv[:, 1, :], bc(lambda_q2)),
            (lamv[:, 2, :], bc(lambda_k1)), (lamv[:, 3, :], bc(lambda_k2)),
            (gsub, bc(g_subln)), (brt, bc(b_router)),
            (wrt, w_router[0].rearrange("(k p) e -> p k e", p=P)),
        ]
        SMALL = 16 * len(small)

        def name_of(u):
            return CHUNKS[ITEMS[u][0]][0]

        def wbuf(c):
            return {WO: W1, WO + 1: HT}.get(c, (W0, W1)[c % 2])

        def wait_wbuf(eng, c):
            if c >= WO:
                eng.wait_ge(projected, len(ITEMS))
            elif c >= 2:
                eng.wait_ge(projected, ITEM_NO[(c - 2, T - 1)] + 1)

        def piece(m):
            n = WIDTH[m // 4]
            return WR[:, m % 4, 0:2 * n].rearrange("p (k n) -> p k n", k=2)

        def wait_piece(eng, m):
            eng.wait_ge(piece_in[m % 4], 16 * sum(len(CHUNKS[j // 4][1]) if j // 4 < WO else 1
                                                  for j in range(m % 4, m + 1, 4)))

        def heads_of(u):
            r = raw[:, u % 4, :]
            if name_of(u) == "kvi":
                return 2, r[:, 0:144].rearrange("p (h d) -> p h d", h=2)[:, :, 0:HD]
            return 8, r.rearrange("p (h d) -> p h d", h=8)

        def is_key(u):
            return name_of(u) in ("kvi", "bk")

        def gain_of(u):
            if name_of(u) == "kvi":
                return gh[:, 3:5, :]
            n = {"aq": 0, "bq": 1, "bk": 2}[name_of(u)]
            return gh[:, n:n + 1, :].to_broadcast([P, 8, HD])

        def wait_raw(eng, u):
            v = u - 4
            if v >= 0 and has_heads(v):
                eng.wait_ge(heads_lo, HEADED.index(v) + 1)

        def wait_stack(eng, u):
            k = HEADED.index(u)
            last = k - 1 if is_key(u) or (k and is_key(HEADED[k - 1])) else k - 2
            if last >= 0:
                st = ("turn_heads", HEADED[last])
                eng.wait_ge(turned, TURN[st] + turns_in(st))

        def turned_heads(u, j):
            t = ITEMS[u][1]
            cols = rows_of(t)
            slot = HEADED.index(u) % 2
            name = name_of(u)
            if name == "kvi":
                return ([stk[:, c, h, :] for h in range(2) for c in range(2)], KAI[:, :, :, cols])
            if name == "bk":
                return ([stk[:, j // 2, 4 * (j % 2) + h, :] for h in range(4)],
                        KB[:, j // 2, :, :][:, 4 * (j % 2):4 * (j % 2) + 4, cols])
            dst = {"iq": IQ, "aq": QA, "bq": QB}[name]
            return [stk[:, slot, 4 * j + h, :] for h in range(4)], dst[:, 4 * j:4 * j + 4, cols]

        def tbank(g):
            return ps[:, TP_BANK + g % 2, :]

        def wait_bank(eng, g):
            if g >= 2:
                eng.wait_ge(turn_read[g % 2], g // 2)

        def wait_turns(eng, g):
            eng.wait_ge(turn_read[0], (g + 1) // 2)
            eng.wait_ge(turn_read[1], g // 2)

        def through(st):
            return TURN[st] + turns_in(st)

        def last_unit(pr):
            kind, t, h = pr
            return 16 * t + (2 * h + 1 if kind == "B" else 8 + h)

        def e_of(n):
            return Ew[:, n % 4, :]

        def e_in(pr):
            n = last_unit(pr)
            return e_of(n - 1 if pr[0] == "B" else n)

        def exp_no(n):
            return SCORE[("score", n)] + 1

        def combo_no(pr):
            return HB * pr[1] + pr[2] + 1

        PER_ROUND = NCH * E

        def is0(i):
            return isinstance(i, int) and i == 0

        def isE(i):
            return isinstance(i, int) and i == E

        def chunks_at(i):
            return range(NG) if is0(i) else range(NG, NCH) if isE(i) else range(NCH)

        def chunk_no(r, i, c):
            if is0(i):
                return PER_ROUND * r + c
            return PER_ROUND * r + NCH * i - ND + (c - NG if isE(i) else c)

        def raw_slot(i, c):
            return (c + ND if is0(i) else c - NG if isE(i) else c) % RAW

        def raw_fill(r, i, c):
            per = PER_ROUND // RAW
            late_slot = 1 if raw_slot(i, c) >= ND else 0
            if is0(i):
                return per * r + (c + ND) // RAW + late_slot
            if isE(i):
                return per * (r + 1)
            return per * r + (NCH // RAW) * i + c // RAW + late_slot

        def gu_done(r, e):
            return chunk_no(r, e, NG - 1) + 1

        def dn_done(r, e):
            if isinstance(e, int) and e == E - 1:
                return PER_ROUND * (r + 1)
            return PER_ROUND * r + NCH * (e + 1) - ND + NCH

        def after(eng, s, value):
            if not (isinstance(value, int) and value <= 0):
                eng.wait_ge(s, value)

        def chunk_src(i, c):
            if c < NG:
                return w_gu[0, i, c * P:(c + 1) * P, :]
            return w_down[0, i - 1].rearrange("(q j p) n -> q p j n", q=ND, j=2)[c - NG]

        def chunk_dst(i, c):
            w = wraw[:, raw_slot(i, c), :]
            return w if c < NG else w.rearrange("p (j n) -> p j n", j=2)

        def more_rounds(eng, one_round):
            most = eng.value_load(cnt[0:1, 0:1], min_val=0, max_val=SEQ)
            with eng.Fori(1, ROUNDS) as r:
                with eng.If(most > r * P):
                    one_round(r)
                eng.nop()

        block = ctx.enter_context(nc.Block())

        @block.sync
        def _(sp):
            for t in range(T):
                sp.dma_start(xs[:, t, :], x[0, rows_of(t), :]).then_inc(x_in[t], 16)
            for m in range(4 * (WO + 2)):
                c, q = m // 4, m % 4
                if m >= 4:
                    sp.wait_ge(w_lo, m - 3)
                src, ranges = (w_in[0], CHUNKS[c][1]) if c < WO else (w_o[0], [(512 * (c - WO), 512)])
                n0 = 0
                for first, n in ranges:
                    sp.dma_start(piece(m)[:, :, n0:n0 + n],
                                 src[2 * q * P:2 * (q + 1) * P, first:first + n]
                                 .rearrange("(k p) n -> p k n", p=P)).then_inc(piece_in[m % 4], 16)
                    n0 += n
            sp.wait_ge(rel_used, N_TOPK_SCORES)
            sp.dma_start(GF, bc(g_ffn)).then_inc(gf_in, 16)
            sp.wait_ge(w_lo, 4 * (WO + 2))
            for t in range(T):
                if t >= 1:
                    sp.wait_ge(logit_ps, t)
                sp.dma_start(xres, x[0, rows_of(t), :]).then_inc(xres_in, 16)
                sp.wait_ge(x1_ok, t + 1)
                sp.dma_start(x1d[rows_of(t), :], x1).then_inc(rows_out, 16)
                if t == T - 1:
                    sp.wait_ge(score_ps, SCORE["all"])
                    for c in range(RAW):
                        sp.dma_start(chunk_dst(0, c), chunk_src(0, c)).then_inc(landed[raw_slot(0, c)], 16)
                sp.wait_ge(h2_ok, t + 1)
                sp.dma_start(hd[rows_of(t), :], h2).then_inc(rows_out, 16)
            sp.wait_ge(logit_ok, T)
            sp.wait_ge(rows_out, 32 * T)
            for h in range(2):
                sp.dma_start(bg_raw[32 * h:32 * h + 32, :], b_gu[0]).then_inc(bg_in, 16)
            sp.dma_start(xbase, x1d.rearrange("(t p) d -> p t d", p=P)).then_inc(xbase_in, 16)
            sp.dma_start(bdn, b_down[0]).then_inc(xbase_in, 16)

            def load_chunk(r, i, c):
                after(sp, chunk_lo, chunk_no(r, i, c) - RAW + 1)
                sp.dma_start(chunk_dst(i, c), chunk_src(i, c)).then_inc(landed[raw_slot(i, c)], 16)

            def stream(r):
                for c in chunks_at(0):
                    if not is0(r) or c >= RAW:
                        load_chunk(r, 0, c)
                with sp.Fori(1, E) as i:
                    for c in chunks_at(i):
                        load_chunk(r, i, c)
                for c in chunks_at(E):
                    load_chunk(r, E, c)

            stream(0)
            more_rounds(sp, stream)
            sp.wait_ge(experts_done, 1)
            for t in range(T):
                if t >= 2:
                    sp.wait_ge(out_ok, t - 1)
                sp.dma_start(yk[:, t % 2], yd[t * P * TOPE:(t + 1) * P * TOPE, :]
                             .rearrange("(p k) d -> p k d", k=TOPE)).then_inc(yk_in[t % 2], 16)
                if t >= 1:
                    sp.wait_ge(out_ok, t)
                    sp.dma_start(out[0, rows_of(t - 1), :], xbase[:, t - 1, :]).then_inc(stored, 16)
            sp.wait_ge(out_ok, T)
            sp.dma_start(out[0, rows_of(T - 1), :], xbase[:, T - 1, :]).then_inc(stored, 16)
            sp.wait_ge(stored, 16 * T)

        @block.gpsimd
        def _(pool):
            steps = [0]

            def link(ins):
                steps[0] += 1
                ins.then_inc(pool_step, 1)
                pool.wait_ge(pool_step, steps[0])

            link(pool.memset(ident, 0.0))
            link(pool.affine_select(out=ident, in_=ident, compare_op=ALU.not_equal, fill=1.0, base=0,
                                    pattern=[[-1, P]], channel_multiplier=1))
            link(pool.tensor_copy(identb, ident))
            link(pool.memset(half, -0.5))
            link(pool.memset(causal, 0.0))
            link(pool.memset(causal[0:CHUNK, CHUNK:P], MASKED))
            link(pool.iota(iota, pattern=[[1, P]], base=0, channel_multiplier=0,
                           allow_small_or_imprecise_dtypes=True))
            link(pool.memset(ones, 1.0))
            link(pool.affine_select(out=tri, in_=ones, compare_op=ALU.is_gt, fill=0.0, base=0,
                                    pattern=[[1, P]], channel_multiplier=-1))
            for j, step in enumerate((1, TOPE)):
                link(pool.iota(r1f[:, j:j + 1], pattern=[[1, 1]], base=0, channel_multiplier=step,
                               allow_small_or_imprecise_dtypes=True))
            link(pool.tensor_copy(r1, r1f))
            for t in range(T):
                link(pool.memset(r2[:, t, 0:1], float(P * t - FAR)))
                link(pool.memset(r2[:, t, 1:2], float(TOPE * (P * t - FAR))))
            link(pool.memset(off[:, 0:1], float(FAR)))
            link(pool.memset(off[:, 1:2], float(TOPE * FAR)))
            link(pool.memset(pick, 0.0))
            for b in (0, E):
                link(pool.affine_select(out=pick, in_=pick, compare_op=ALU.not_equal, fill=1.0, base=-b,
                                        pattern=[[-1, E + 1]], channel_multiplier=1))
            link(pool.memset(ke, 0.0))
            link(pool.memset(zero, 0))
            pool.memset(rows, 0).then_inc(const, 1)
            pool.wait_ge(x_mean, 1)
            pool.tensor_tensor(rstd[:, 4, 0:T], ss[:, 4, 0:T], half[:, 0:T], ALU.pow).then_inc(x_root, 1)

            for st in PLAN:
                if st[0] == "norm" and st[1] in NORMED:
                    u = st[1]
                    _, view = heads_of(u)
                    pool.wait_ge(scaled, NORMED.index(u) + 1)
                    pool.tensor_tensor(view, view, gain_of(u), ALU.mult).then_inc(gained, 1)
                elif st[0] == "sums" and st[1] in NORMED:
                    u = st[1]
                    n, view = heads_of(u)
                    k = NORMED.index(u)
                    pool.wait_ge(raw_ok, u + 1)
                    if k >= 2:
                        pool.wait_ge(summed, k - 1)
                    pool.tensor_tensor(sq[:, k % 2, 0:n * HD].rearrange("p (h d) -> p h d", h=n), view,
                                       view, ALU.mult).then_inc(squared, 1)
                    pool.wait_ge(summed, k + 1)
                    pool.tensor_tensor(rstd[:, k % 4, 0:n], ss[:, k % 4, 0:n], half[:, 0:n],
                                       ALU.pow).then_inc(rooted, 1)
                elif st[0] == "mix":
                    pool.wait_ge(yss, st[1] + 1)
                    pool.tensor_tensor(rstd[:, 4, 0:HB], ss[:, 4, 0:HB], half[:, 0:HB], ALU.pow) \
                        .then_inc(yroot, 1)
                elif st[0] == "post_mean":
                    pool.wait_ge(x1_mean, st[1] + 1)
                    pool.tensor_tensor(tss[:, 2:3], tss[:, 1:2], half[:, 0:1], ALU.pow).then_inc(x1_root, 1)

            pool.wait_ge(logit_ok, T)
            pool.memset(xg, 0.0).then_inc(xg_clear, 1)
            pool.wait_ge(xg_clear, 1)
            pool.wait_ge(rows_out, 32 * T)

            def gather(r, j):
                pool.wait_ge(idx_ok, 33 * r + j + 1)
                after(pool, xT_ps, 66 * r + 2 * j)
                for n, (a, b) in enumerate(((rows[:, 2:3], rows[:, 1:2]), (rows[:, 1:2], rows[:, 0:1]),
                                            (rows[:, 0:1], idx2[:, 1:2]))):
                    after(pool, row_ok, 99 * r + 3 * j + n)
                    pool.tensor_tensor(a, b, zero, ALU.add).then_inc(row_ok, 1)
                pool.indirect_dma_start(xg, None, hd, bass.IndirectOffsetOnAxis(ap=idx2[:, 0:1], axis=0),
                                        bounds_check=SEQ - 1, oob_is_err=False).then_inc(gathered, 16)

            def scatter(r, e, col):
                pool.wait_ge(yrow_ok, E * r + e + 1)
                pool.tensor_tensor(passed[:, col:col + 1], zero, zero, ALU.add)
                pool.indirect_dma_start(yd, bass.IndirectOffsetOnAxis(ap=rows[:, col:col + 1], axis=0), ysb,
                                        None, bounds_check=SEQ * TOPE - 1, oob_is_err=False) \
                    .then_inc(scattered, 16)
                pool.wait_ge(scattered, 16 * (E * r + e + 1))

            def pool_round(r):
                for j in range(3):
                    gather(r, j)
                with pool.Fori(2, E) as i:
                    scatter(r, i - 2, 2)
                    gather(r, i + 1)
                scatter(r, E - 2, 2)
                scatter(r, E - 1, 1)

            pool_round(0)
            more_rounds(pool, pool_round)
            pool.memset(passed[:, 0:1], 0).then_inc(experts_done, 1)

        @block.scalar
        def _(act):
            for dst, src in small:
                act.dma_start(dst, src, allow_slow_non_contiguous=True).then_inc(small_in, 16)
            for t in range(T):
                act.wait_ge(x_in[t], 16)
                act.activation(squares[:, t, :], xs[:, t, :], ACT.Square, accum_out=ss[:, 3, t:t + 1]) \
                   .then_inc(x_sum, 1)
            act.wait_ge(angles, 1)
            act.activation(sinr[:, :, HALF:ROT], ang, ACT.Sin).then_inc(sines, 1)
            act.activation(cosr[:, :, 0:HALF], cyc, ACT.Sin).then_inc(sines, 1)
            act.wait_ge(lam_in, 1)
            act.activation(lams[:, 0:2], lams[:, 2:4], ACT.Exp).then_inc(lam_exp, 1)

            for st in PLAN:
                kind = st[0]
                if kind == "turn_h":
                    k, g = st[1], TURN[st]
                    act.wait_ge(turned, g + 1)
                    act.wait_ge(small_in, SMALL)
                    act.activation(HT[:, 0, k, :], tbank(g), ACT.Copy, scale=gcol[:, k:k + 1]) \
                       .then_inc(hi_ok, 1)
                elif kind == "split_w":
                    m = st[1]
                    c, q = m // 4, m % 4
                    wait_piece(act, m)
                    wait_wbuf(act, c)
                    act.activation(wbuf(c)[:, 0, 2 * q:2 * q + 2, 0:WIDTH[c]], piece(m), ACT.Copy) \
                       .then_inc(w_hi, 1)
                elif kind == "proj":
                    u = st[1]
                    act.wait_ge(projected, u + 1)
                    wait_raw(act, u)
                    n = WIDTH[ITEMS[u][0]]
                    dst = raw[:, u % 4, 0:n] if has_heads(u) else VB[:, ITEMS[u][1], :]
                    act.activation(dst, ps[:, ACC + u % 2, 0:n], ACT.Copy).then_inc(raw_ok, 1)
                elif kind == "split_heads":
                    u = st[1]
                    k = HEADED.index(u)
                    n, view = heads_of(u)
                    act.wait_ge(roped, k + 1)
                    wait_stack(act, u)
                    if is_key(u):
                        act.activation(stk[:, 0, 0:n, :].rearrange("p h (c d) -> p h c d", c=2),
                                       view.unsqueeze(2).to_broadcast([P, n, 2, HD]), ACT.Copy) \
                           .then_inc(heads_hi, 1)
                    else:
                        act.activation(stk[:, k % 2, 0:n, 0:HD], view, ACT.Copy).then_inc(heads_hi, 1)
                elif kind == "turn_heads":
                    u = st[1]
                    if name_of(u) == "bq":
                        act.wait_ge(score_ps, N_TOPK_SCORES)
                    if name_of(u) == "bk":
                        act.wait_ge(projected, ITEM_NO[(WO - 2, T - 1)] + 1)
                    for j in range(turns_in(st)):
                        g = TURN[st] + j
                        act.wait_ge(turned, g + 1)
                        dst = turned_heads(u, j)[1]
                        src = tbank(g)
                        src = src.rearrange("p (a b n) -> p a b n", a=2, b=2) if name_of(u) == "kvi" \
                            else src.rearrange("p (h n) -> p h n", h=4)
                        act.activation(dst, src, ACT.Copy).then_inc(turn_read[g % 2], 1)
                elif kind == "iscore":
                    v, w = SCORE[st], keys_of(st[1])
                    act.wait_ge(score_ps, v + 1)
                    if v >= 2:
                        act.wait_ge(rel_used, v - 1)
                    act.activation(rel[:, v % 2, 0:w], ps[:, S_BANK + v % 2, 0:w], ACT.Relu) \
                       .then_inc(score_read, 1)
                elif kind == "score":
                    n, v = st[1], SCORE[st]
                    t, j = n // 16, n % 16
                    w = keys_of(t)
                    act.wait_ge(max_ok, n + 1)
                    if n < 4:
                        act.wait_ge(heads_lo, len(HEADED))
                    elif (n - 4) % 16 < 8 and n % 2:
                        act.wait_ge(combined, combo_no(("B", (n - 4) // 16, (n - 4) % 16 // 2)))
                    else:
                        pr = ("B", (n - 4) // 16, (n - 4) % 16 // 2) if (n - 4) % 16 < 8 \
                            else ("A", (n - 4) // 16, (n - 4) % 16 - 8)
                        act.wait_ge(turned, TURN[("turn_p", pr)] + 1)
                    if t >= 2 and j == 0:
                        act.wait_ge(y_ok, t - 1)
                    act.activation(e_of(n)[:, 0:w], ps[:, S_BANK + v % 2, 0:w], ACT.Exp,
                                   bias=nmax[:, t % 2, j:j + 1], accum_out=lsum[:, t % 2, j:j + 1]) \
                       .then_inc(score_read, 1)
                elif kind == "turn_p" and TURN[st] % 2 == 0:
                    i, g, w = PROD[st], TURN[st], keys_of(st[1][1])
                    act.wait_ge(turned, g + 1)
                    if i >= 2:
                        act.wait_ge(values_ok, i - 1)
                    act.activation(PT[:, i % 2, 0:w], tbank(g)[:, 0:w], ACT.Copy).then_inc(turn_read[0], 1)
                elif kind == "turn_y":
                    t = st[1]
                    for j in range(2):
                        g = TURN[st] + j
                        act.wait_ge(turned, g + 1)
                        if t >= 1:
                            act.wait_ge(acc_ps, t)
                        act.activation(yT[:, 0, 4 * j:4 * j + 4, :],
                                       tbank(g).rearrange("p (k n) -> p k n", k=4), ACT.Copy) \
                           .then_inc(hi_ok, 1)
                elif kind == "post":
                    t = st[1]
                    act.wait_ge(x1_ok, t + 1)
                    act.activation(y, x1, ACT.Square, accum_out=tss[:, 0:1]).then_inc(x1_sq, 1)
                elif kind == "turn_h2":
                    g = TURN[st]
                    if g % 2 == 0:
                        j = 0
                    else:
                        j = 1
                    act.wait_ge(turned, g + j + 1)
                    act.activation(h2T[:, 4 * j:4 * j + 4, :], tbank(g + j)
                                   .rearrange("p (k n) -> p k n", k=4), ACT.Copy).then_inc(turn_read[0], 1)

            act.wait_ge(gates_in, 1)
            act.activation(gate, gate, ACT.Exp).then_inc(gates_exp, 1)
            act.wait_ge(bg_in, 32)
            act.activation(bgs, bg_raw, ACT.Copy).then_inc(bg_hi, 1)

            def split_hi(r, i, c):
                n = chunk_no(r, i, c)
                act.wait_ge(landed[raw_slot(i, c)], 16 * raw_fill(r, i, c))
                after(act, chunk_used, n - HL + 1)
                act.activation(whl[:, c % HL, 0, :], wraw[:, raw_slot(i, c), :], ACT.Copy) \
                   .then_inc(chunk_hi, 1)

            def turn_x_hi(r, j):
                after(act, chunk_used, PER_ROUND * r if is0(j) else gu_done(r, j - 1))
                for b in range(2):
                    act.wait_ge(xT_ps, 66 * r + 2 * j + b + 1)
                    act.activation(xT[:, 0, 4 * b:4 * b + 4, :],
                                   ps[:, TP + b, :].rearrange("p (k n) -> p k n", k=4), ACT.Copy) \
                       .then_inc(xT_hi, 1)

            def turn_a_hi(r, e):
                after(act, chunk_used, PER_ROUND * r if is0(e) else dn_done(r, e - 1))
                for b in range(2):
                    act.wait_ge(aT_ps, 64 * r + 2 * e + b + 1)
                    act.activation(aT[:, 0, 4 * b:4 * b + 4, :],
                                   ps[:, TP + b, :].rearrange("p (k n) -> p k n", k=4), ACT.Copy) \
                       .then_inc(aT_hi, 1)

            def sigmoid(r, e):
                act.wait_ge(glu_ok, E * r + e + 1)
                act.activation(acts[:, 2, :], acts[:, 0, :], ACT.Sigmoid, scale=ALPHA).then_inc(sig_ok, 1)

            def y_rows(r, e):
                act.wait_ge(chunk_used, dn_done(r, e))
                after(act, scattered, 16 * (E * r + e))
                act.activation(ysb.rearrange("p (a n) -> p a n", a=2), ps[:, DN:DN + 2, :], ACT.Copy) \
                   .then_inc(yrow_ok, 1)

            def act_body(r, i, first=False):
                if not first:
                    y_rows(r, i - 2)
                turn_a_hi(r, i - 1)
                for c in range(NCH - 1):
                    split_hi(r, i, c)
                turn_x_hi(r, i + 1)
                sigmoid(r, i)
                split_hi(r, i, NCH - 1)

            def act_round(r):
                turn_x_hi(r, 0)
                for c in range(NG):
                    split_hi(r, 0, c)
                turn_x_hi(r, 1)
                sigmoid(r, 0)
                act_body(r, 1, first=True)
                act_body(r, 2)
                with act.Fori(3, E) as i:
                    act_body(r, i)
                y_rows(r, E - 2)
                turn_a_hi(r, E - 1)
                for c in chunks_at(E):
                    split_hi(r, E, c)
                y_rows(r, E - 1)

            act_round(0)
            more_rounds(act, act_round)

        @block.vector
        def _(dve):
            steps = [0]

            def link(ins):
                steps[0] += 1
                ins.then_inc(dve_step, 1)
                dve.wait_ge(dve_step, steps[0])

            dve.wait_ge(small_in, SMALL)
            link(dve.tensor_copy(posf, posi))
            for j in range(HALF):
                ins = dve.tensor_scalar(ang[:, :, j], posf, float(INV_FREQ[j]), None, ALU.mult)
            link(ins)
            for scale in (2.0 ** 15, 1.0):
                link(dve.tensor_scalar(cyc, ang, 1.0 / (2 * math.pi * scale), ROUND_BY, ALU.mult, ALU.add))
                link(dve.tensor_scalar(cyc, cyc, ROUND_BY, None, ALU.subtract))
                for part in TWO_PI:
                    link(dve.scalar_tensor_tensor(out=ang, in0=cyc, scalar=-part * scale, in1=ang,
                                                  op0=ALU.mult, op1=ALU.add))
            link(dve.tensor_scalar(ang, ang, PI_BELOW, -PI_BELOW, ALU.min, ALU.max))
            link(dve.scalar_tensor_tensor(out=cyc, in0=ang, scalar=-1.0, in1=ang, op0=ALU.mult, op1=ALU.max))
            dve.tensor_scalar(cyc, cyc, -1.0, math.pi / 2, ALU.mult, ALU.add).then_inc(angles, 1)
            link(dve.tensor_tensor(lamv[:, 0:2, :], lamv[:, 0:2, :], lamv[:, 2:4, :], ALU.mult))
            dve.tensor_reduce(lams[:, 2:4], lamv[:, 0:2, :], AX.X, ALU.add).then_inc(lam_in, 1)
            link(dve.tensor_scalar(gh[:, 0:2, :], gh[:, 0:2, :], HD ** -0.5, None, ALU.mult))
            link(dve.tensor_scalar(gsub, gsub, 1.0 - LAM_INIT, None, ALU.mult))
            dve.wait_ge(x_sum, T)
            dve.tensor_scalar(ss[:, 4, 0:T], ss[:, 3, 0:T], 1.0 / D, EPS, ALU.mult, ALU.add).then_inc(x_mean, 1)
            dve.wait_ge(lam_exp, 1)
            link(dve.tensor_tensor(lams[:, 4:5], lams[:, 1:2], lams[:, 0:1], ALU.subtract))
            link(dve.tensor_scalar(lams[:, 4:5], lams[:, 4:5], -LAM_INIT, None, ALU.add))
            dve.wait_ge(x_root, 1)
            for t in range(T):
                dve.tensor_scalar(xs[:, t, :], xs[:, t, :], rstd[:, 4, t:t + 1], None, ALU.mult) \
                   .then_inc(h_ok, 1)
            dve.wait_ge(sines, 2)
            dve.tensor_scalar(sinr[:, :, 0:HALF], sinr[:, :, HALF:ROT], -1.0, None, ALU.mult)
            link(dve.tensor_copy(cosr[:, :, HALF:ROT], cosr[:, :, 0:HALF]))

            for st in PLAN:
                kind = st[0]
                if kind == "turn_h":
                    k, g = st[1], TURN[st]
                    dve.wait_ge(hi_ok, SPLIT[st] + 1)
                    dve.scalar_tensor_tensor(out=HT[:, 1, k, :], in0=tbank(g), scalar=gcol[:, k:k + 1],
                                             in1=HT[:, 0, k, :].bitcast(F32), op0=ALU.mult,
                                             op1=ALU.subtract).then_inc(turn_read[g % 2], 1)
                elif kind == "split_w":
                    m = st[1]
                    c, q = m // 4, m % 4
                    b = wbuf(c)[:, :, 2 * q:2 * q + 2, 0:WIDTH[c]]
                    dve.wait_ge(w_hi, m + 1)
                    dve.tensor_tensor(b[:, 1], piece(m), b[:, 0].bitcast(F32), ALU.subtract).then_inc(w_lo, 1)
                elif kind == "sums":
                    u = st[1]
                    t = ITEMS[u][1]
                    if name_of(u) == "kvi":
                        dve.wait_ge(raw_ok, u + 1)
                        dve.tensor_scalar(iw[:, t, :], raw[:, u % 4, C_IW:C_IW + HI], (HI * HD) ** -0.5,
                                          None, ALU.mult)
                        dve.tensor_copy(VA[:, t, :], raw[:, u % 4, C_AV:C_AV + HD])
                    if u in NORMED:
                        k = NORMED.index(u)
                        n, _ = heads_of(u)
                        dve.wait_ge(squared, k + 1)
                        if k >= 4:
                            dve.wait_ge(rooted, k - 3)
                        link(dve.tensor_reduce(ss[:, k % 4, 0:n],
                                               sq[:, k % 2, 0:n * HD].rearrange("p (h d) -> p h d", h=n),
                                               AX.X, ALU.add))
                        dve.tensor_scalar(ss[:, k % 4, 0:n], ss[:, k % 4, 0:n], 1.0 / HD, EPS, ALU.mult,
                                          ALU.add).then_inc(summed, 1)
                elif kind == "norm" and st[1] in NORMED:
                    u = st[1]
                    k = NORMED.index(u)
                    n, view = heads_of(u)
                    dve.wait_ge(rooted, k + 1)
                    dve.tensor_tensor(view, view, rstd[:, k % 4, 0:n].unsqueeze(2).to_broadcast([P, n, HD]),
                                      ALU.mult).then_inc(scaled, 1)
                elif kind == "rope":
                    u = st[1]
                    t = ITEMS[u][1]
                    n, view = heads_of(u)
                    if u in NORMED:
                        dve.wait_ge(gained, NORMED.index(u) + 1)
                    else:
                        dve.wait_ge(raw_ok, u + 1)

                    def over_heads(table):
                        return table.unsqueeze(1).to_broadcast([P, n, table.shape[-1]])

                    dve.tensor_tensor(rp[:, 0, 0:n, :], view[:, :, 0:ROT], over_heads(cosr[:, t, :]), ALU.mult)
                    dve.tensor_tensor(rp[:, 1, 0:n, 0:HALF], view[:, :, HALF:ROT],
                                      over_heads(sinr[:, t, 0:HALF]), ALU.mult)
                    link(dve.tensor_tensor(rp[:, 1, 0:n, HALF:ROT], view[:, :, 0:HALF],
                                           over_heads(sinr[:, t, HALF:ROT]), ALU.mult))
                    dve.tensor_tensor(view[:, :, 0:ROT], rp[:, 0, 0:n, :], rp[:, 1, 0:n, :], ALU.add) \
                       .then_inc(roped, 1)
                elif kind == "split_heads":
                    u = st[1]
                    k = HEADED.index(u)
                    n, view = heads_of(u)
                    dve.wait_ge(heads_hi, k + 1)
                    if is_key(u):
                        for half_ in range(2):
                            cols = slice(half_ * HD, (half_ + 1) * HD)
                            ins = dve.tensor_tensor(stk[:, 1, 0:n, cols], view,
                                                    stk[:, 0, 0:n, cols].bitcast(F32), ALU.subtract)
                        ins.then_inc(heads_lo, 1)
                    else:
                        dve.tensor_tensor(stk[:, k % 2, 0:n, HD:P], view,
                                          stk[:, k % 2, 0:n, 0:HD].bitcast(F32), ALU.subtract) \
                           .then_inc(heads_lo, 1)
                elif kind == "iscore":
                    _, t, h = st
                    v, w = SCORE[st], keys_of(t)
                    dst = work[:, t - 1, 0:w]
                    dve.wait_ge(score_read, v + 1)
                    if h == 0:
                        ins = dve.tensor_scalar(dst, rel[:, v % 2, 0:w], iw[:, t, 0:1], None, ALU.mult)
                    else:
                        ins = dve.scalar_tensor_tensor(out=dst, in0=rel[:, v % 2, 0:w],
                                                       scalar=iw[:, t, h:h + 1], in1=dst, op0=ALU.mult,
                                                       op1=ALU.add)
                    ins.then_inc(rel_used, 1)
                    dve.wait_ge(rel_used, v + 1)
                    if h == HI - 1:
                        link(dve.memset(work[0:CHUNK, t - 1, w - CHUNK:w], MASKED))
                elif kind == "topk":
                    _, t, r = st
                    w = keys_of(t)
                    link(dve.max(top, work[:, t - 1, 0:w]))
                    link(dve.match_replace(work[:, t - 1, 0:w], top, work[:, t - 1, 0:w], TAKEN))
                elif kind == "mask":
                    t = st[1]
                    w = keys_of(t)
                    dve.tensor_scalar(maskA[:, t, 0:w], work[:, t - 1, 0:w], TAKEN / 2, MASKED, ALU.is_gt,
                                      ALU.mult).then_inc(mask_ok, 1)
                elif kind == "score":
                    n, v = st[1], SCORE[st]
                    t, j = n // 16, n % 16
                    dve.wait_ge(score_ps, v + 1)
                    if t >= 2 and j == 0:
                        dve.wait_ge(score_read, exp_no(16 * (t - 1) - 1))
                    dve.tensor_reduce(nmax[:, t % 2, j:j + 1], ps[:, S_BANK + v % 2, 0:keys_of(t)], AX.X,
                                      ALU.max, negate=True).then_inc(max_ok, 1)
                elif kind == "turn_p":
                    pr = st[1]
                    i, g, w = PROD[st], TURN[st], keys_of(pr[1])
                    if pr[0] == "B":
                        _, t, h = pr
                        n = last_unit(pr)
                        dve.wait_ge(score_read, exp_no(n))
                        rat = ratio[:, 0, h:h + 1]
                        link(dve.reciprocal(rat, lsum[:, t % 2, 2 * h + 1:2 * h + 2]))
                        link(dve.scalar_tensor_tensor(out=rat, in0=rat, scalar=lams[:, 4:5],
                                                      in1=lsum[:, t % 2, 2 * h:2 * h + 1], op0=ALU.mult,
                                                      op1=ALU.mult))
                        dve.scalar_tensor_tensor(out=e_of(n - 1)[:, 0:w], in0=e_of(n)[:, 0:w], scalar=rat,
                                                 in1=e_of(n - 1)[:, 0:w], op0=ALU.mult, op1=ALU.add) \
                           .then_inc(combined, 1)
                    if g % 2:
                        dve.wait_ge(turned, g + 1)
                        if i >= 2:
                            dve.wait_ge(values_ok, i - 1)
                        dve.tensor_copy(PT[:, i % 2, 0:w], tbank(g)[:, 0:w]).then_inc(turn_read[1], 1)
                elif kind == "mix":
                    t = st[1]
                    dve.wait_ge(values_ok, (HB + HA) * (t + 1))
                    if t >= 1:
                        dve.wait_ge(x1_sq, t)
                    link(dve.reciprocal(rl, lsum[:, t % 2, :]))
                    yB = y[:, 512:1024].rearrange("p (h d) -> p h d", h=HB)
                    dve.tensor_tensor(y[:, 0:512].rearrange("p (h d) -> p h d", h=HA),
                                      ps[:, OA, :].rearrange("p (h d) -> p h d", h=HA),
                                      rl[:, 8:16].unsqueeze(2).to_broadcast([P, HA, HD]), ALU.mult)
                    link(dve.tensor_tensor(yB, ps[:, OB, :].rearrange("p (h d) -> p h d", h=HB),
                                           rl[:, 0:8:2].unsqueeze(2).to_broadcast([P, HB, 2 * HD]), ALU.mult))
                    link(dve.tensor_tensor(ps[:, OB, :], y[:, 512:1024], y[:, 512:1024], ALU.mult))
                    link(dve.tensor_reduce(ss[:, 4, 0:HB], ps[:, OB, :].rearrange("p (h d) -> p h d", h=HB),
                                           AX.X, ALU.add))
                    dve.tensor_scalar(ss[:, 4, 0:HB], ss[:, 4, 0:HB], 1.0 / (2 * HD), EPS, ALU.mult,
                                      ALU.add).then_inc(yss, 1)
                elif kind == "mix_norm":
                    t = st[1]
                    dve.wait_ge(yroot, t + 1)
                    yB = y[:, 512:1024].rearrange("p (h d) -> p h d", h=HB)
                    link(dve.tensor_tensor(yB, yB, rstd[:, 4, 0:HB].unsqueeze(2)
                                           .to_broadcast([P, HB, 2 * HD]), ALU.mult))
                    dve.tensor_tensor(yB, yB, gsub.unsqueeze(1).to_broadcast([P, HB, 2 * HD]), ALU.mult) \
                       .then_inc(y_ok, 1)
                elif kind == "turn_y":
                    for j in range(2):
                        g = TURN[st] + j
                        dve.wait_ge(hi_ok, SPLIT[st] + j + 1)
                        dve.tensor_tensor(yT[:, 1, 4 * j:4 * j + 4, :],
                                          tbank(g).rearrange("p (k n) -> p k n", k=4),
                                          yT[:, 0, 4 * j:4 * j + 4, :].bitcast(F32), ALU.subtract) \
                           .then_inc(turn_read[g % 2], 1)
                elif kind == "post":
                    t = st[1]
                    dve.wait_ge(acc_ps, t + 1)
                    dve.wait_ge(xres_in, 16 * (t + 1))
                    if t >= 1:
                        dve.wait_ge(rows_out, 32 * t)
                    dve.tensor_tensor(x1.rearrange("p (a n) -> p a n", a=2), ps[:, ACC:ACC + 2, :],
                                      xres.rearrange("p (a n) -> p a n", a=2), ALU.add).then_inc(x1_ok, 1)
                elif kind == "post_mean":
                    t = st[1]
                    dve.wait_ge(x1_sq, t + 1)
                    dve.tensor_scalar(tss[:, 1:2], tss[:, 0:1], 1.0 / D, EPS, ALU.mult, ALU.add) \
                       .then_inc(x1_mean, 1)
                elif kind == "post_norm":
                    t = st[1]
                    dve.wait_ge(x1_root, t + 1)
                    if t == 0:
                        dve.wait_ge(gf_in, 16)
                    dve.scalar_tensor_tensor(out=h2, in0=x1, scalar=tss[:, 2:3], in1=GF, op0=ALU.mult,
                                             op1=ALU.mult).then_inc(h2_ok, 1)
                elif kind == "turn_h2":
                    g = TURN[st]
                    j = 1 if g % 2 == 0 else 0
                    dve.wait_ge(turned, g + j + 1)
                    dve.tensor_copy(h2T[:, 4 * j:4 * j + 4, :], tbank(g + j)
                                    .rearrange("p (k n) -> p k n", k=4)).then_inc(turn_read[1], 1)
                elif kind == "route":
                    t = st[1]
                    dve.wait_ge(logit_ps, t + 1)
                    dve.tensor_tensor(lg[:, t, :], ps[:, ACC, 0:E], brt, ALU.add).then_inc(logit_ok, 1)

            dve.wait_ge(logit_ok, T)
            for t in range(T):
                link(dve.max(top8[:, t, :], lg[:, t, :]))
                ins = dve.max_index(idx8[:, t, :], top8[:, t, :], lg[:, t, :])
            link(ins)
            dve.tensor_tensor(gate, top8[:, :, 0:TOPE], top8[:, :, 0:1].to_broadcast([P, T, TOPE]),
                              ALU.subtract).then_inc(gates_in, 1)
            link(dve.tensor_copy(idxf, idx8[:, :, 0:TOPE]))
            for t in range(T):
                ins = dve.tensor_tensor(one[:, t], iota[:, 0:E].unsqueeze(1).to_broadcast([P, TOPE, E]),
                                        idxf[:, t, :].unsqueeze(2).to_broadcast([P, TOPE, E]), ALU.is_equal)
            link(ins)
            for t in range(T):
                ins = dve.tensor_reduce(selm[:, t, :], one[:, t].rearrange("p k e -> p e k"), AX.X, ALU.add)
            link(ins)
            dve.tensor_copy(selb, selm).then_inc(picked, 1)
            link(dve.scalar_tensor_tensor(out=kef, in0=one[:, :, 2, :], scalar=2.0, in1=one[:, :, 1, :],
                                          op0=ALU.mult, op1=ALU.add))
            link(dve.scalar_tensor_tensor(out=ke[:, :, 0:E], in0=one[:, :, 3, :], scalar=3.0, in1=kef,
                                          op0=ALU.mult, op1=ALU.add))
            dve.wait_ge(rank_ps, 1)
            link(dve.memset(rank, -1.0))
            link(dve.scalar_tensor_tensor(out=kef, in0=ps[:, TP + 1, 0:T * E].rearrange("p (t e) -> p t e", t=T),
                                          scalar=1.0, in1=selm, op0=ALU.add, op1=ALU.mult))
            link(dve.tensor_scalar(rank[:, :, 0:E], kef, -1.0, None, ALU.add))
            link(dve.tensor_reduce(cmax, ps[:, TP + 1, T * E:(T + 1) * E], AX.X, ALU.max))
            dve.tensor_copy(cnt, cmax).then_inc(routed, 1)

            def slots(r, j):
                after(dve, idx_ps, 33 * r + j)
                for t in range(T):
                    ins = dve.tensor_scalar(oh[:, t, :], iota, rank[:, t, bass.ds(j, 1)], None, ALU.is_equal)
                ins.then_inc(slots_ok, 1)

            def find_rows(r, j):
                dve.wait_ge(idx_ps, 33 * r + j + 1)
                after(dve, gathered, 16 * (33 * r + j))
                after(dve, row_ok, 3 * (33 * r + j))
                dve.tensor_tensor(idx2, ps[:, TP + 1, 0:2], off, ALU.add).then_inc(idx_ok, 1)
                after(dve, bias_mm, E * r + j)
                dve.tensor_copy(sel, pick[:, bass.ds(j, 1)].to_broadcast([64, P])).then_inc(pick_ok, 1)

            slots(0, 0)
            dve.wait_ge(gates_exp, 1)
            link(dve.tensor_reduce(gsum, gate, AX.X, ALU.add))
            link(dve.reciprocal(gsum, gsum))
            link(dve.tensor_tensor(gate, gate, gsum.unsqueeze(2).to_broadcast([P, T, TOPE]), ALU.mult))
            for t in range(T):
                ins = dve.tensor_tensor(onek[:, t], one[:, t],
                                        gate[:, t, :].unsqueeze(2).to_broadcast([P, TOPE, E]), ALU.mult)
            link(ins)
            for t in range(T):
                ins = dve.tensor_reduce(gden[:, t, :], onek[:, t].rearrange("p k e -> p e k"), AX.X, ALU.add)
            ins.then_inc(gden_ok, 1)
            dve.wait_ge(bg_hi, 1)
            dve.tensor_tensor(bgs[32:64, :], bg_raw[32:64, :], bgs[32:64, :].bitcast(F32), ALU.subtract) \
               .then_inc(bg_ok, 1)
            dve.wait_ge(gd_ps, 1)
            dve.tensor_copy(gdT, ps[0:E, TP, :]).then_inc(gd_ok, 1)

            def split_lo(r, i, c):
                n = chunk_no(r, i, c)
                dve.wait_ge(chunk_hi, n + 1)
                dve.tensor_tensor(whl[:, c % HL, 1, :], wraw[:, raw_slot(i, c), :],
                                  whl[:, c % HL, 0, :].bitcast(F32), ALU.subtract).then_inc(chunk_lo, 1)

            def turn_x_lo(r, j):
                for b in range(2):
                    dve.wait_ge(xT_hi, 66 * r + 2 * j + b + 1)
                    dve.tensor_tensor(xT[:, 1, 4 * b:4 * b + 4, :],
                                      ps[:, TP + b, :].rearrange("p (k n) -> p k n", k=4),
                                      xT[:, 0, 4 * b:4 * b + 4, :].bitcast(F32), ALU.subtract) \
                       .then_inc(xT_lo, 1)

            def turn_a_lo(r, e):
                for b in range(2):
                    dve.wait_ge(aT_hi, 64 * r + 2 * e + b + 1)
                    dve.tensor_tensor(aT[:, 1, 4 * b:4 * b + 4, :],
                                      ps[:, TP + b, :].rearrange("p (k n) -> p k n", k=4),
                                      aT[:, 0, 4 * b:4 * b + 4, :].bitcast(F32), ALU.subtract) \
                       .then_inc(aT_lo, 1)

            def glu(r, e):
                dve.wait_ge(chunk_used, gu_done(r, e))
                after(dve, act_ok, E * r + e)
                dve.tensor_scalar(acts[:, 0, :].rearrange("p (a n) -> p a n", a=2), ps[:, GU:GU + 2, :],
                                  LIMIT, None, ALU.min).then_inc(glu_ok, 1)

            def lin(r, e):
                dve.tensor_scalar(acts[:, 1, :].rearrange("p (a n) -> p a n", a=2), ps[:, GU + 2:GU + 4, :],
                                  LIMIT, -LIMIT, ALU.min, ALU.max).then_inc(lin_ok, 1)
                dve.wait_ge(lin_ok, E * r + e + 1)
                dve.scalar_tensor_tensor(out=acts[:, 1, :], in0=acts[:, 1, :], scalar=1.0, in1=acts[:, 0, :],
                                         op0=ALU.add, op1=ALU.mult).then_inc(prod_ok, 1)

            def activate(r, e):
                dve.wait_ge(prod_ok, E * r + e + 1)
                dve.wait_ge(sig_ok, E * r + e + 1)
                after(dve, aT_ps, 64 * r + 2 * e)
                dve.tensor_tensor(acts[:, 3, :], acts[:, 1, :], acts[:, 2, :], ALU.mult).then_inc(act_ok, 1)

            def start_of(r):
                find_rows(r, 0)
                slots(r, 1)

            def dve_round(r):
                if not is0(r):
                    dve.tensor_scalar(iota, iota, float(P), None, ALU.add).then_inc(round_step, 1)
                    dve.wait_ge(round_step, r)
                    slots(r, 0)
                start_of(r)
                if is0(r):
                    dve.wait_ge(xbase_in, 32)
                    for t in range(T):
                        for h in range(2):
                            dst = xbase[:, t, 512 * h:512 * h + 512]
                            dve.wait_ge(bterm_ps, 2 * t + h + 1)
                            dve.tensor_tensor(dst, ps[:, DN + h, :], dst, ALU.add).then_inc(base_ok, 1)
                for c in range(NG):
                    split_lo(r, 0, c)
                    if c == 0:
                        turn_x_lo(r, 0)
                    if c == HL:
                        find_rows(r, 1)
                glu(r, 0)
                turn_x_lo(r, 1)
                lin(r, 0)
                activate(r, 0)
                dve_body(r, 1)
                with dve.Fori(2, E) as i:
                    dve_body(r, i)
                turn_a_lo(r, E - 1)
                for c in chunks_at(E):
                    split_lo(r, E, c)

            def dve_body(r, i):
                slots(r, i + 1)
                turn_a_lo(r, i - 1)
                for c in range(NCH - 1):
                    split_lo(r, i, c)
                    if c == HL:
                        find_rows(r, i + 1)
                glu(r, i)
                turn_x_lo(r, i + 1)
                lin(r, i)
                split_lo(r, i, NCH - 1)
                activate(r, i)

            dve_round(0)
            more_rounds(dve, dve_round)
            dve.wait_ge(base_ok, 2 * T)
            for t in range(T):
                dve.wait_ge(yk_in[t % 2], 16 * (t // 2 + 1))
                for k in range(TOPE):
                    ins = dve.scalar_tensor_tensor(out=xbase[:, t, :], in0=yk[:, t % 2, k, :],
                                                   scalar=gate[:, t, k:k + 1], in1=xbase[:, t, :],
                                                   op0=ALU.mult, op1=ALU.add)
                    if k == TOPE - 1:
                        ins.then_inc(out_ok, 1)
                    else:
                        link(ins)

        @block.tensor
        def _(pe):
            def three(dst, a, b, k_first, k_last):
                pe.matmul(dst, a[0], b[0], start=k_first, stop=False)
                pe.matmul(dst, a[0], b[1], start=False, stop=False)
                return pe.matmul(dst, a[1], b[0], start=False, stop=k_last)

            def turn(g, sources):
                wait_bank(pe, g)
                for j, s_ in enumerate(sources):
                    ins = pe.transpose(tbank(g)[:, j * P:(j + 1) * P], s_, ident)
                ins.then_inc(turned, 1)

            pe.wait_ge(const, 1)
            pe.wait_ge(h_ok, T)
            for st in PLAN:
                kind = st[0]
                if kind == "turn_h":
                    turn(TURN[st], [xs[:, t, st[1] * P:(st[1] + 1) * P] for t in range(T)])
                elif kind == "proj":
                    u = st[1]
                    c, t = ITEMS[u]
                    if u == 0:
                        wait_turns(pe, KD)
                    if u >= 2:
                        pe.wait_ge(raw_ok, u - 1)
                    dst = ps[:, ACC + u % 2, 0:WIDTH[c]]
                    for k in range(KD):
                        if k % 2 == 0:
                            pe.wait_ge(w_lo, 4 * c + k // 2 + 1)
                        ins = three(dst, [HT[:, a, k, rows_of(t)] for a in range(2)],
                                    [wbuf(c)[:, b, k, 0:WIDTH[c]] for b in range(2)], k == 0, k == KD - 1)
                    ins.then_inc(projected, 1)
                elif kind == "turn_heads":
                    u = st[1]
                    pe.wait_ge(heads_lo, HEADED.index(u) + 1)
                    for j in range(turns_in(st)):
                        turn(TURN[st] + j, [s_.bitcast(F32) for s_ in turned_heads(u, j)[0]])
                elif kind == "iscore":
                    _, t, h = st
                    v, w = SCORE[st], keys_of(t)
                    if v == 0:
                        wait_turns(pe, through(("turn_heads", ITEM_NO[(1, T - 1)])))
                    if v >= 2:
                        pe.wait_ge(score_read, v - 1)
                    dst = ps[:, S_BANK + v % 2, 0:w]
                    pe.matmul(dst, IQ[:, h, rows_of(t)], KAI[:, 0, 0, 0:w], start=True, stop=False)
                    pe.matmul(dst, IQ[:, h, rows_of(t)], KAI[:, 0, 1, 0:w], start=False, stop=True) \
                      .then_inc(score_ps, 1)
                elif kind == "score":
                    n, v = st[1], SCORE[st]
                    t, j = n // 16, n % 16
                    w = keys_of(t)
                    if n == 0:
                        wait_turns(pe, through(("turn_heads", HEADED[-1])))
                    pe.wait_ge(score_read, v - 1)
                    dst = ps[:, S_BANK + v % 2, 0:w]
                    if j < 8:
                        q, keys = QB[:, j, rows_of(t)], [KB[:, a, j, 0:w] for a in range(2)]
                    else:
                        q, keys = QA[:, j - 8, rows_of(t)], [KAI[:, 1, a, 0:w] for a in range(2)]
                    pe.matmul(dst, q, keys[0], start=True, stop=False)
                    if j < 8 or t == 0:
                        pe.matmul(dst[:, w - P:w], identb, causal, start=False, stop=False)
                    else:
                        if j == 8:
                            pe.wait_ge(mask_ok, t)
                        pe.matmul(dst, identb, maskA[:, t, 0:w], start=False, stop=False)
                    pe.matmul(dst, q, keys[1], start=False, stop=True).then_inc(score_ps, 1)
                elif kind == "turn_p":
                    pr = st[1]
                    if pr[0] == "B":
                        pe.wait_ge(combined, combo_no(pr))
                    else:
                        pe.wait_ge(score_read, exp_no(last_unit(pr)))
                    turn(TURN[st], [e_in(pr)[:, rows_of(b)] for b in range(pr[1] + 1)])
                elif kind == "values":
                    pr = st[1]
                    which, t, h = pr
                    i, g = PROD[("turn_p", pr)], TURN[("turn_p", pr)]
                    pe.wait_ge(turn_read[g % 2], g // 2 + 1)
                    if which == "B" and h == 0 and t >= 1:
                        pe.wait_ge(yss, t)
                    for b in range(t + 1):
                        if which == "B":
                            dst, val = ps[:, OB, h * P:(h + 1) * P], VB[:, b, h * P:(h + 1) * P]
                        else:
                            dst, val = ps[:, OA, h * HD:(h + 1) * HD], VA[:, b, :]
                        ins = pe.matmul(dst, PT[:, i % 2, rows_of(b)], val, start=(b == 0), stop=(b == t))
                    ins.then_inc(values_ok, 1)
                elif kind == "turn_y":
                    t = st[1]
                    pe.wait_ge(y_ok, t + 1)
                    for j in range(2):
                        turn(TURN[st] + j, [y[:, (4 * j + k) * P:(4 * j + k + 1) * P] for k in range(4)])
                elif kind == "out_proj":
                    _, t, k = st
                    if k == 0:
                        wait_turns(pe, through(("turn_y", t)))
                        pe.wait_ge(w_lo, 4 * (WO + 2))
                        if t >= 1:
                            pe.wait_ge(logit_ok, t)
                    for h in range(2):
                        ins = three(ps[:, ACC + h, :], [yT[:, a, k, :] for a in range(2)],
                                    [wbuf(WO + h)[:, b, k, :] for b in range(2)], k == 0, k == KD - 1)
                    if k == KD - 1:
                        ins.then_inc(acc_ps, 1)
                elif kind == "turn_h2":
                    t = st[1]
                    pe.wait_ge(h2_ok, t + 1)
                    for j in range(2):
                        turn(TURN[st] + j, [h2[:, (4 * j + k) * P:(4 * j + k + 1) * P] for k in range(4)])
                elif kind == "route":
                    t = st[1]
                    wait_turns(pe, through(("turn_h2", t)))
                    for k in range(KD):
                        ins = pe.matmul(ps[:, ACC, 0:E], h2T[:, k, :], wrt[:, k, :], start=(k == 0),
                                        stop=(k == KD - 1))
                    ins.then_inc(logit_ps, 1)

            pe.wait_ge(picked, 1)
            for t in range(T):
                dst = ps[:, TP + 1, t * E:(t + 1) * E]
                for b in range(t):
                    pe.matmul(dst, ones, selb[:, b, :], start=(b == 0), stop=False)
                pe.matmul(dst, tri, selb[:, t, :], start=(t == 0), stop=True)
            for b in range(T):
                ins = pe.matmul(ps[:, TP + 1, T * E:(T + 1) * E], ones, selb[:, b, :], start=(b == 0),
                                stop=(b == T - 1))
            ins.then_inc(rank_ps, 1)

            def find(r, j):
                pe.wait_ge(slots_ok, 33 * r + j + 1)
                if is0(r) and is0(j):
                    pe.wait_ge(routed, 1)
                else:
                    pe.wait_ge(idx_ok, 33 * r + j)
                dst = ps[:, TP + 1, 0:2]
                for t in range(T):
                    pe.matmul(dst, oh[:, t, :], r1, start=(t == 0), stop=False)
                    pe.matmul(dst[:, 1:2], oh[:, t, :], ke[:, t, bass.ds(j, 1)], start=False, stop=False)
                    ins = pe.matmul(dst, oh[:, t, :], r2[:, t, :], start=False, stop=(t == T - 1))
                ins.then_inc(idx_ps, 1)

            def turn_x(r, j):
                pe.wait_ge(gathered, 16 * (33 * r + j + 1))
                for b in range(2):
                    for k in range(4):
                        ins = pe.transpose(ps[:, TP + b, k * P:(k + 1) * P],
                                           xg[:, (4 * b + k) * P:(4 * b + k + 1) * P], ident)
                    ins.then_inc(xT_ps, 1)

            def turn_a(r, e):
                pe.wait_ge(act_ok, E * r + e + 1)
                pe.wait_ge(xT_lo, 66 * r + 2 * e + 4)
                for b in range(2):
                    for k in range(4):
                        ins = pe.transpose(ps[:, TP + b, k * P:(k + 1) * P],
                                           acts[:, 3, (4 * b + k) * P:(4 * b + k + 1) * P], ident)
                    ins.then_inc(aT_ps, 1)

            def chunk_products(r, i, c, a, banks):
                pe.wait_ge(chunk_lo, chunk_no(r, i, c) + 1)
                nj = len(a[0])
                w = whl[:, c % HL].rearrange("p s (j n) -> p s j n", j=nj)
                first, last = (False, False) if c < NG - 1 else (False, c in (NG - 1, NCH - 1))
                for j in range(nj):
                    for n, (x_, b) in enumerate(((0, 0), (0, 1), (1, 0))):
                        for q, bank in enumerate(banks):
                            start = c == NG and j == 0 and n == 0
                            ins = pe.matmul(bank, a[x_][j], w[:, b, j, 512 * q:512 * q + 512], start=start,
                                            stop=last and j == nj - 1 and n == 2)
                ins.then_inc(chunk_used, 1)

            def gate_up(r, i, between=None):
                pe.wait_ge(pick_ok, 33 * r + i + 1)
                after(pe, lin_ok, E * r + i)
                banks = [ps[:, GU + q, :] for q in range(4)]
                for q, bank in enumerate(banks):
                    ins = pe.matmul(bank, sel, bgs[:, 512 * q:512 * q + 512], start=True, stop=False)
                ins.then_inc(bias_mm, 1)
                pe.wait_ge(xT_lo, 66 * r + 2 * i + 2)
                for c in range(NG):
                    chunk_products(r, i, c, [[xT[:, a, c, :]] for a in range(2)], banks)
                    if c == HL - 1:
                        between()

            def down(r, i):
                banks = [ps[:, DN + q, :] for q in range(2)]
                pe.wait_ge(aT_lo, 64 * r + 2 * i)
                for c in range(NG, NCH):
                    k = 2 * (c - NG)
                    if c == NG:
                        if is0(r) and isinstance(i, int) and i == 1:
                            pe.wait_ge(base_ok, 2 * T)
                        after(pe, yrow_ok, E * r + i - 1)
                    chunk_products(r, i, c, [[aT[:, a, k + j, :] for j in range(2)] for a in range(2)], banks)

            def find_next(r, j):
                after(pe, aT_lo, 64 * r + 2 * (j - 1) if not is0(j - 1) else 64 * r)
                find(r, j)

            def pe_body(r, i):
                gate_up(r, i, lambda: find_next(r, i + 1))
                pe.wait_ge(idx_ok, 33 * r + i + 2)
                turn_x(r, i + 1)
                down(r, i)
                turn_a(r, i)

            def pe_round(r):
                if not is0(r):
                    pe.wait_ge(aT_lo, 64 * r)
                find(r, 0)
                if is0(r):
                    pe.wait_ge(gden_ok, 1)
                    for t in range(T):
                        ins = pe.transpose(ps[0:E, TP, rows_of(t)], gden[:, t, :], ident)
                    ins.then_inc(gd_ps, 1)
                    pe.wait_ge(gd_ok, 1)
                    pe.wait_ge(xbase_in, 32)
                    for t in range(T):
                        for h in range(2):
                            after(pe, base_ok, 2 * t + h - 1)
                            pe.matmul(ps[:, DN + h, :], gdT[:, rows_of(t)], bdn[:, 512 * h:512 * h + 512],
                                      start=True, stop=True).then_inc(bterm_ps, 1)
                    pe.wait_ge(bg_ok, 1)
                pe.wait_ge(idx_ok, 33 * r + 1)
                turn_x(r, 0)
                pe.wait_ge(xT_lo, 66 * r + 2)
                gate_up(r, 0, lambda: find(r, 1))
                pe.wait_ge(idx_ok, 33 * r + 2)
                turn_x(r, 1)
                turn_a(r, 0)
                pe_body(r, 1)
                with pe.Fori(2, E) as i:
                    pe_body(r, i)
                down(r, E)

            pe_round(0)
            more_rounds(pe, pe_round)


_INS = ['x', 'positions', 'g_attn', 'w_in', 'g_qa', 'g_ka', 'g_idx_k', 'lambda_q1', 'lambda_k1',
        'lambda_q2', 'lambda_k2', 'g_qb', 'g_kb', 'g_subln', 'w_o', 'g_ffn', 'w_router', 'b_router',
        'w_gu', 'b_gu', 'w_down', 'b_down']
_OUTS = [((1, SEQ, D), 'float32')]


def kernel(**inputs):
    import concourse.bacc as _bacc
    from concourse.bass_utils import run_bass_kernel_spmd as _run

    nc = _bacc.Bacc("TRN2", target_bir_lowering=False, num_devices=1)
    arrays, args = {}, []
    for name in _INS:
        a = np.ascontiguousarray(inputs[name])
        arrays[f"in_{name}_dram"] = a
        args.append(nc.dram_tensor(f"in_{name}_dram", a.shape, mybir.dt.from_np(a.dtype), kind="ExternalInput").ap())
    for i, (shape, dtype) in enumerate(_OUTS):
        dt = mybir.dt.from_np(np.dtype(dtype))
        args.append(nc.dram_tensor(f"out_{i}_dram", shape, dt, kind="ExternalOutput").ap())
    build(nc, *args)
    r = _run(nc, [arrays], core_ids=[0])
    return r.results[0]["out_0_dram"]
```

```python
import math
from contextlib import ExitStack

import numpy as np

import concourse.bass as bass
from concourse import mybir

ALU = mybir.AluOpType
ACT = mybir.ActivationFunctionType
AX = mybir.AxisListType
F32 = mybir.dt.float32
F32R = mybir.dt.float32r
BF16 = mybir.dt.bfloat16
I32 = mybir.dt.int32
U32 = mybir.dt.uint32

P = 128
SEQ, D = 512, 1024
T = SEQ // P
KD = D // P
CHUNK = 64
ROPE_THETA = 500000.0
EPS = 1e-6
HA, HI, HB, HD = 8, 8, 4, 64
ROT = HD // 4
HALF = ROT // 2
TOPK = min(256, SEQ // 4)
E, TOPE, DE = 32, 4, 1024
LIMIT, ALPHA = 7.0, 1.702
LAM_INIT = 0.8 - 0.6 * math.exp(0.0)
FAR = 2 ** 14
INV_FREQ = np.array([ROPE_THETA ** (-j / ROT) for j in range(0, ROT, 2)]).astype(np.float32)
ROUND_BY = 1.5 * 2.0 ** 23
TWO_PI = (201 / 32, 253 / 128 * 2.0 ** -10, 2 * math.pi - 201 / 32 - 253 / 128 * 2.0 ** -10)
PI_BELOW = 3.1415925
MASKED = -1e30
TAKEN = -3e38

O_AQ, O_AK, O_AV, O_IQ = 0, 512, 576, 640
O_IK, O_IW, O_BQ, O_BK, O_BV = 1152, 1216, 1224, 1736, 2248
CHUNKS = [("iq", [(O_IQ, 512)]), ("kvi", [(O_IK, 72), (O_AK, 128)]), ("aq", [(O_AQ, 512)]),
          ("bv", [(O_BV, 512)]), ("bq", [(O_BQ, 512)]), ("bk", [(O_BK, 512)])]
C_IW, C_AV = 64, 136
WO = len(CHUNKS)
WIDTH = [sum(n for _, n in c[1]) for c in CHUNKS] + [512, 512]

ITEMS = [(c, t) for c in range(len(CHUNKS)) for t in range(T) if not (CHUNKS[c][0] == "iq" and t == 0)]
ITEM_NO = {it: u for u, it in enumerate(ITEMS)}
ROUNDS_TOPK = TOPK // 8
AHEAD = 5
POOL_SPLITS = range(8, 4 * WO)


def has_heads(u):
    return CHUNKS[ITEMS[u][0]][0] != "bv"


def keys_of(t):
    return P * (t + 1)


def make_plan():
    pieces = [("split_w", m) for m in range(4 * (WO + 2))]
    plan = []
    for k in range(0, KD, 2):
        plan += [("turn_h", k), ("turn_h", k + 1), pieces.pop(0)]
    plan += [("setup",)]
    scores = [("iscore", t, h) for t in range(1, T) for h in range(HI)]
    search = [("topk", t, r) for t in range(1, T) for r in range(ROUNDS_TOPK)]

    def next_search(n):
        for _ in range(n):
            if search and ("iscore", search[0][1], HI - 1) in plan:
                plan.append(search.pop(0))

    units = [(t, j) for t in range(T) for j in range(16)]

    def product_of(n):
        if not 0 <= n < len(units):
            return None
        t, j = units[n]
        if j < 8:
            return ("B", t, j // 2) if j % 2 else None
        return ("A", t, j - 8)

    late = {-5: ["mix_b"], -3: ["mix_norm"], 3: ["mix_a"], 4: ["turn_y"], 13: ["post"],
            14: ["post_mean"], 15: ["post_norm"], 16: ["turn_h2"], 17: ["route"]}

    def attend(n):
        if n == len(units) + 5:
            plan.append(("biases",))
        if n < len(units):
            t, j = units[n]
            if t >= 1 and j == 7:
                while search and search[0][1] <= t:
                    plan.append(search.pop(0))
                plan.append(("mask", t))
            plan.append(("score", n))
            if t >= 1:
                next_search(n >= 22 and n % 16 >= 6)
        if pieces and n % 2:
            plan.append(pieces.pop(0))
        if product_of(n - 1) and product_of(n - 1)[0] == "B":
            plan.append(("combine", product_of(n - 1)))
        if product_of(n - 2):
            plan.append(("turn_p", product_of(n - 2)))
        if product_of(n - 3):
            plan.append(("values", product_of(n - 3)))
        for t in range(T):
            lag = n - 16 * (t + 1)
            if 5 <= lag < 5 + KD:
                plan.append(("out_proj", t, lag - 5))
            for kind in {**late, -5: [], -3: [], 1: ["mix_b"], 3: ["mix_norm", "mix_a"]}.get(lag, []) \
                    if t == 0 else late.get(lag, []):
                plan.append((kind, t))

    attended = list(range(len(units) + 18))
    n_items = len(ITEMS)
    for s in range(n_items + 3):
        norm = 0 <= s - 2 < n_items and has_heads(s - 2)
        if norm:
            plan.append(("norm", s - 2))
        if s < n_items:
            while pieces and pieces[0][1] <= 4 * ITEMS[s][0] + 4 + ITEMS[s][1] and pieces[0][1] < 4 * WO:
                plan.append(pieces.pop(0))
        if 0 <= s - 1 < n_items and has_heads(s - 1):
            plan.append(("sums", s - 1))
        if norm:
            plan.append(("rope", s - 2))
        if 0 <= s - 3 < n_items and has_heads(s - 3):
            plan.append(("turn_heads", s - 3))
        if norm:
            plan.append(("split_heads", s - 2))
        if s < n_items:
            plan.append(("proj", s))
        if s >= 10:
            for _ in range(4):
                if scores:
                    plan.append(scores.pop(0))
            if s < n_items:
                next_search(3)
        if s >= n_items:
            for _ in range(AHEAD):
                attend(attended.pop(0))
    while attended:
        attend(attended.pop(0))
    return plan


PLAN = make_plan()


def number(kinds, count=lambda st: 1):
    at, out = 0, {}
    for st in PLAN:
        if st[0] in kinds:
            out[st] = at
            at += count(st)
    out["all"] = at
    return out


def turns_in(st):
    if st[0] == "turn_heads":
        name = CHUNKS[ITEMS[st[1]][0]][0]
        return {"iq": 2, "aq": 2, "bq": 2, "kvi": 1, "bk": 4}[name]
    return {"turn_h": 1, "turn_p": 1, "turn_y": 2, "turn_h2": 2}[st[0]]


TURN = number(("turn_h", "turn_heads", "turn_p", "turn_y", "turn_h2"), turns_in)
SPLIT = number(("turn_h", "turn_y"), turns_in)
SCORE = number(("iscore", "score"))
PROD = number(("turn_p",))
HEADED = [u for u in range(len(ITEMS)) if has_heads(u)]
NORMED = [u for u in HEADED if CHUNKS[ITEMS[u][0]][0] != "iq"]
N_TOPK_SCORES = HI * (T - 1)

NG, ND = KD, KD // 2
NCH = NG + ND
EARLY = 2
TURN_AT, COPY_AT, FIND_AT = 0, 3, 3
RAW, HL = 6, 4
ROUNDS = SEQ // P


def build(nc, x, positions, g_attn, w_in, g_qa, g_ka, g_idx_k, lambda_q1, lambda_k1,
          lambda_q2, lambda_k2, g_qb, g_kb, g_subln, w_o, g_ffn, w_router, b_router,
          w_gu, b_gu, w_down, b_down, out):
    with ExitStack() as ctx:
        at = {"free": 16512}

        def place(name, shape, dt, offset=None):
            size = int(np.prod(shape[1:])) * mybir.dt.size(dt)
            size = -(-size // 32) * 32
            if offset is None:
                offset = at["free"]
                at["free"] += size
            return nc.alloc_sbuf_tensor_at(name, shape, dt, offset=offset).ap()

        def sem(name):
            return ctx.enter_context(nc.semaphore(name))

        base = at["free"]
        W0 = place("W0", [P, 2, KD, 512], F32R)
        QA = place("QA", [P, HA, SEQ], F32R)
        W1 = place("W1", [P, 2, KD, 512], F32R)
        HT = place("HT", [P, 2, KD, SEQ], F32R)
        QB = place("QB", [P, 2 * HB, SEQ], F32R)
        KAI = place("KAI", [P, 2, 2, SEQ], F32R)
        stk = place("stk", [P, 2, 8, P], F32R)
        WR = place("WR", [P, 4, 1024], F32)
        VB = place("VB", [P, T, 512], F32)
        VA = place("VA", [P, T, HD], F32)
        raw = place("raw", [P, 4, 512], F32)
        sq = place("sq", [P, 2, 512], F32)
        work = place("work", [P, T - 1, SEQ], F32)
        rel = place("rel", [P, 2, SEQ], F32)
        maskA = place("maskA", [P, T, SEQ], BF16)
        kept = at["free"]
        xs = place("xs", [P, T, D], F32, offset=base + 32768)
        squares = place("squares", [P, T, D], F32, offset=base + 49152)
        KB = W0
        IQ = QB
        Ew = raw
        PT = sq
        y = WR[:, 0, :]
        yB = y[:, 512:1024].rearrange("p (h d) -> p h d", h=HB)
        xres = WR[:, 1, :]
        h2 = WR[:, 2, :]
        x1 = WR[:, 3, :]
        yT = stk
        h2T = xres.rearrange("p (k n) -> p k n", k=KD)
        GF = rel.rearrange("p a b -> p (a b)")
        wraw = place("wraw", [P, RAW, 2048], F32, offset=base)
        whl = place("whl", [P, HL, 2, 2048], F32R, offset=base + 49152)
        o_qb = base + 49152 + 65536
        bgs = place("bgs", [2 * E, 3072], F32R, offset=o_qb)
        bg_raw = place("bg_raw", [2 * E, 3072], F32, offset=o_qb + 12288)
        aT = place("aT", [P, 2, KD, P], F32R, offset=o_qb + 16384)
        xT = place("xT", [P, 2, KD, P], F32R, offset=o_qb + 24576)
        acts = place("acts", [P, 4, 1024], F32, offset=o_qb + 32768)
        oh = place("oh", [P, T, P], BF16, offset=o_qb + 49152)
        ysb = place("ysb", [P, D], F32, offset=o_qb + 50176)
        xg = place("xg", [P, D], F32, offset=o_qb + 54272)
        rank = place("rank", [P, T, E + 1], F32, offset=o_qb + 63488)
        selm = place("selm", [P, T, E], F32, offset=o_qb + 64032)
        selb = place("selb", [P, T, E], BF16, offset=o_qb + 64544)
        sel_gu = place("sel_gu", [2 * E, P], F32R, offset=o_qb + 64800)
        sel_dn = place("sel_dn", [2 * E, P], F32R, offset=o_qb + 65312)
        at["free"] = kept
        one = place("one", [P, T, TOPE, E], F32, offset=o_qb + 58368)
        onek = place("onek", [P, T, TOPE, E], F32, offset=o_qb + 60416)
        gden = place("gden", [P, T, E], F32, offset=o_qb + 62464)
        kef = place("kef", [P, T, E], F32, offset=o_qb + 62976)
        ident = place("ident", [P, P], F32)
        identb = place("identb", [P, P], BF16)
        causal = place("causal", [P, P], BF16)
        gcol = place("gcol", [P, KD], F32)
        gh = place("gh", [P, 5, HD], F32)
        gsub = place("gsub", [P, 2 * HD], F32)
        posi = place("posi", [P, T], I32)
        posf = place("posf", [P, T], F32)
        ang = place("ang", [P, T, HALF], F32)
        cyc = place("cyc", [P, T, HALF], F32)
        cosr = place("cosr", [P, T, ROT], F32)
        sinr = place("sinr", [P, T, ROT], F32)
        lamv = place("lamv", [P, 4, HD], F32)
        lams = place("lams", [P, 8], F32)
        half = place("half", [P, 16], F32)
        ss = place("ss", [P, 5, 8], F32)
        rstd = place("rstd", [P, 5, 8], F32)
        rp = place("rp", [P, 2, 8, ROT], F32)
        xroot = place("xroot", [P, T], F32)
        iw = place("iw", [P, T, HI], F32)
        top = place("top", [P, 8], F32)
        nmax = place("nmax", [P, 2, 16], F32)
        lsum = place("lsum", [P, 2, 16], F32)
        ratio = place("ratio", [P, HB], F32)
        rl = place("rl", [P, 16], F32)
        tss = place("tss", [P, 4], F32)
        wrt = place("wrt", [P, KD, E], F32)
        brt = place("brt", [P, E], F32)
        lg = place("lg", [P, T, E], F32)
        top8 = place("top8", [P, T, 8], F32)
        idx8 = place("idx8", [P, T, 8], U32)
        idxf = place("idxf", [P, T, TOPE], F32)
        gate = place("gate", [P, T, TOPE], F32)
        gsum = place("gsum", [P, T], F32)
        iota = place("iota", [P, P], F32)
        tri = place("tri", [P, P], BF16)
        ones = place("ones", [P, P], BF16)
        tokf = place("tokf", [P, 1], F32)
        tok1 = place("tok1", [P, T], BF16)
        tokg = place("tokg", [P, T, E + 1, 3], BF16)
        tok128 = place("tok128", [P, T], BF16)
        idx = place("idx", [P, 1], U32)
        gslot = place("gslot", [P, E + 1], F32)
        mark = place("mark", [P, 1], F32)
        rows = place("rows", [P, 3], U32)
        zero = place("zero", [P, 1], U32)
        passed = place("passed", [P, 3], U32)
        cmax = place("cmax", [P, 1], F32)
        cnt = place("cnt", [P, 1], I32)
        pick = place("pick", [2 * E, E + 1], F32)
        assert at["free"] <= nc.sbuf_usable_end, at["free"]

        ps = ctx.enter_context(nc.psum_tensor("ps", [P, 8, 512], F32))
        S_BANK, TP_BANK, ACC, OB, OA = 0, 2, 4, 6, 7
        GU, DN, TP = 0, 4, 6

        hd = nc.dram_tensor("h_rows", (SEQ, D), F32).ap()

        x_in = [sem(f"x_in{t}") for t in range(T)]
        gcol_in = sem("gcol_in")
        small_in = sem("small_in")
        piece_in = [sem(f"piece_in{s}") for s in range(4)]
        xres_in = sem("xres_in")
        gf_in = sem("gf_in")
        const = sem("const")
        pool_step = sem("pool_step")
        dve_step = sem("dve_step")
        x_sum = sem("x_sum")
        x_mean = sem("x_mean")
        x_root = sem("x_root")
        angles = sem("angles")
        sines = sem("sines")
        lam_in = sem("lam_in")
        lam_exp = sem("lam_exp")
        turned = sem("turned")
        turn_read = [sem("turn_read0"), sem("turn_read1")]
        hi_ok = sem("hi_ok")
        w_hi = sem("w_hi")
        w_lo = sem("w_lo")
        projected = sem("projected")
        raw_ok = sem("raw_ok")
        squared = sem("squared")
        summed = sem("summed")
        rooted = sem("rooted")
        scaled = sem("scaled")
        gained = sem("gained")
        roped = sem("roped")
        heads_hi = sem("heads_hi")
        heads_lo = sem("heads_lo")
        score_ps = sem("score_ps")
        score_read = sem("score_read")
        rel_used = sem("rel_used")
        mask_ok = sem("mask_ok")
        max_ok = sem("max_ok")
        combined = sem("combined")
        values_ok = sem("values_ok")
        rl_ok = sem("rl_ok")
        y_squared = sem("y_squared")
        yss = sem("yss")
        yb_ok = sem("yb_ok")
        yroot = sem("yroot")
        y_ok = sem("y_ok")
        acc_ps = sem("acc_ps")
        x1_ok = sem("x1_ok")
        x1_sq = sem("x1_sq")
        x1_mean = sem("x1_mean")
        x1_root = sem("x1_root")
        h2_ok = sem("h2_ok")
        logit_ps = sem("logit_ps")
        logit_ok = sem("logit_ok")
        rows_out = sem("rows_out")
        gates_in = sem("gates_in")
        gates_exp = sem("gates_exp")
        picked = sem("picked")
        rank_ps = sem("rank_ps")
        routed = sem("routed")
        bg_in = sem("bg_in")
        bg_hi = sem("bg_hi")
        bg_ok = sem("bg_ok")
        landed = [sem(f"landed{s}") for s in range(RAW)]
        chunk_hi = sem("chunk_hi")
        chunk_lo = sem("chunk_lo")
        chunk_used = sem("chunk_used")
        slots_ok = sem("slots_ok")
        pick_ok = sem("pick_ok")
        idx_ps = sem("idx_ps")
        idx_ok = sem("idx_ok")
        gates_ok = sem("gates_ok")
        gate_ps = sem("gate_ps")
        gslot_ok = sem("gslot_ok")
        row_ok = sem("row_ok")
        sel_ok = sem("sel_ok")
        down_bias_mm = sem("down_bias_mm")
        xg_clear = sem("xg_clear")
        gathered = sem("gathered")
        xT_ps = sem("xT_ps")
        xT_hi = sem("xT_hi")
        xT_lo = sem("xT_lo")
        bias_mm = sem("bias_mm")
        glu_ok = sem("glu_ok")
        sig_ok = sem("sig_ok")
        lin_ok = sem("lin_ok")
        prod_ok = sem("prod_ok")
        act_ok = sem("act_ok")
        aT_ps = sem("aT_ps")
        aT_hi = sem("aT_hi")
        aT_lo = sem("aT_lo")
        yrow_ok = sem("yrow_ok")
        scattered = sem("scattered")
        round_step = sem("round_step")

        def rows_of(t):
            return slice(t * P, (t + 1) * P)

        def bc(row):
            return row[0].partition_broadcast(P)

        small = [
            (posi, positions[0].rearrange("(t p) -> p t", p=P)),
            (gh[:, 0, :], bc(g_qa)), (gh[:, 1, :], bc(g_qb)), (gh[:, 2, :], bc(g_kb)),
            (gh[:, 3, :], bc(g_idx_k)), (gh[:, 4, :], bc(g_ka)),
            (lamv[:, 0, :], bc(lambda_q1)), (lamv[:, 1, :], bc(lambda_q2)),
            (lamv[:, 2, :], bc(lambda_k1)), (lamv[:, 3, :], bc(lambda_k2)),
            (gsub, bc(g_subln)), (brt, bc(b_router)),
            (wrt, w_router[0].rearrange("(k p) e -> p k e", p=P)),
        ]
        SMALL = 16 * len(small)

        def name_of(u):
            return CHUNKS[ITEMS[u][0]][0]

        def wbuf(c):
            return {WO: W1, WO + 1: HT}.get(c, (W0, W1)[c % 2])

        def split_w_lo(eng, m):
            c, q = m // 4, m % 4
            b = wbuf(c)[:, :, 2 * q:2 * q + 2, 0:WIDTH[c]]
            eng.wait_ge(w_hi, m + 1)
            eng.tensor_tensor(b[:, 1], piece(m), b[:, 0].bitcast(F32), ALU.subtract).then_inc(w_lo, 1)

        def wait_wbuf(eng, c):
            if c >= WO:
                eng.wait_ge(projected, len(ITEMS))
            elif c >= 2:
                eng.wait_ge(projected, ITEM_NO[(c - 2, T - 1)] + 1)

        def piece(m):
            n = WIDTH[m // 4]
            return WR[:, m % 4, 0:2 * n].rearrange("p (k n) -> p k n", k=2)

        def wait_piece(eng, m):
            eng.wait_ge(piece_in[m % 4], 16 * sum(len(CHUNKS[j // 4][1]) if j // 4 < WO else 1
                                                  for j in range(m % 4, m + 1, 4)))

        def heads_of(u):
            r = raw[:, u % 4, :]
            if name_of(u) == "kvi":
                return 2, r[:, 0:144].rearrange("p (h d) -> p h d", h=2)[:, :, 0:HD]
            return 8, r.rearrange("p (h d) -> p h d", h=8)

        def is_key(u):
            return name_of(u) in ("kvi", "bk")

        def gain_of(u):
            if name_of(u) == "kvi":
                return gh[:, 3:5, :]
            n = {"aq": 0, "bq": 1, "bk": 2}[name_of(u)]
            return gh[:, n:n + 1, :].to_broadcast([P, 8, HD])

        def wait_raw(eng, u):
            v = u - 4
            if v >= 0 and has_heads(v):
                eng.wait_ge(heads_lo, HEADED.index(v) + 1)

        def wait_stack(eng, u):
            k = HEADED.index(u)
            last = k - 1 if is_key(u) or (k and is_key(HEADED[k - 1])) else k - 2
            if last >= 0:
                st = ("turn_heads", HEADED[last])
                eng.wait_ge(turned, TURN[st] + turns_in(st))

        def turned_heads(u, j):
            t = ITEMS[u][1]
            cols = rows_of(t)
            slot = HEADED.index(u) % 2
            name = name_of(u)
            if name == "kvi":
                return ([stk[:, c, h, :] for h in range(2) for c in range(2)], KAI[:, :, :, cols])
            if name == "bk":
                return ([stk[:, j // 2, 4 * (j % 2) + h, :] for h in range(4)],
                        KB[:, j // 2, :, :][:, 4 * (j % 2):4 * (j % 2) + 4, cols])
            dst = {"iq": IQ, "aq": QA, "bq": QB}[name]
            return [stk[:, slot, 4 * j + h, :] for h in range(4)], dst[:, 4 * j:4 * j + 4, cols]

        def tbank(g):
            return ps[:, TP_BANK + g % 2, :]

        def wait_bank(eng, g):
            if g >= 2:
                eng.wait_ge(turn_read[g % 2], g // 2)

        def wait_turns(eng, g):
            eng.wait_ge(turn_read[0], (g + 1) // 2)
            eng.wait_ge(turn_read[1], g // 2)

        def through(st):
            return TURN[st] + turns_in(st)

        def last_unit(pr):
            kind, t, h = pr
            return 16 * t + (2 * h + 1 if kind == "B" else 8 + h)

        def e_of(n):
            return rel[:, 0, rows_of(n % 4)] if n < 16 else Ew[:, n % 4, :]

        def pt_of(st):
            i = PROD[st]
            return rel[:, 1, rows_of(i % 2)] if st[1][1] == 0 else PT[:, i % 2, :]

        def e_in(pr):
            n = last_unit(pr)
            return e_of(n - 1 if pr[0] == "B" else n)

        def exp_no(n):
            return SCORE[("score", n)] + 1

        def combo_no(pr):
            return HB * pr[1] + pr[2] + 1

        PER_ROUND = NCH * E

        def is0(i):
            return isinstance(i, int) and i == 0

        def isE(i):
            return isinstance(i, int) and i == E

        def chunks_at(i):
            return range(NG) if is0(i) else range(NG, NCH) if isE(i) else range(NCH)

        def chunk_no(r, i, c):
            if is0(i):
                return PER_ROUND * r + c
            return PER_ROUND * r + NCH * i - ND + (c - NG if isE(i) else c)

        def raw_slot(i, c):
            return (c + ND if is0(i) else c - NG if isE(i) else c) % RAW

        def raw_fill(r, i, c):
            per = PER_ROUND // RAW
            late_slot = 1 if raw_slot(i, c) >= ND else 0
            if is0(i):
                return per * r + (c + ND) // RAW + late_slot
            if isE(i):
                return per * (r + 1)
            return per * r + (NCH // RAW) * i + c // RAW + late_slot

        def gu_done(r, e):
            return chunk_no(r, e, NG - 1) + 1

        def dn_done(r, e):
            if isinstance(e, int) and e == E - 1:
                return PER_ROUND * (r + 1)
            return PER_ROUND * r + NCH * (e + 1) - ND + NCH

        def after(eng, s, value):
            if not (isinstance(value, int) and value <= 0):
                eng.wait_ge(s, value)

        def chunk_src(i, c):
            if c < NG:
                return w_gu[0, i, c * P:(c + 1) * P, :]
            return w_down[0, i - 1].rearrange("(q j p) n -> q p j n", q=ND, j=2)[c - NG]

        def chunk_dst(i, c):
            w = wraw[:, raw_slot(i, c), :]
            return w if c < NG else w.rearrange("p (j n) -> p j n", j=2)

        def split_hi(act, r, i, c):
            n = chunk_no(r, i, c)
            act.wait_ge(landed[raw_slot(i, c)], 16 * raw_fill(r, i, c))
            after(act, chunk_used, n - HL + 1)
            act.activation(whl[:, c % HL, 0, :], wraw[:, raw_slot(i, c), :], ACT.Copy) \
               .then_inc(chunk_hi, 1)

        def split_lo(eng, r, i, c):
            eng.wait_ge(chunk_hi, chunk_no(r, i, c) + 1)
            eng.tensor_tensor(whl[:, c % HL, 1, :], wraw[:, raw_slot(i, c), :],
                              whl[:, c % HL, 0, :].bitcast(F32), ALU.subtract).then_inc(chunk_lo, 1)

        def more_rounds(eng, one_round):
            most = eng.value_load(cnt[0:1, 0:1], min_val=0, max_val=SEQ)
            with eng.Fori(1, ROUNDS) as r:
                with eng.If(most > r * P):
                    one_round(r)
                eng.nop()

        block = ctx.enter_context(nc.Block())

        @block.sync
        def _(sp):
            for t in range(T):
                sp.dma_start(xs[:, t, :], x[0, rows_of(t), :]).then_inc(x_in[t], 16)
            for m in range(4 * (WO + 2)):
                c, q = m // 4, m % 4
                if m >= 4:
                    sp.wait_ge(w_lo, m - 3)
                src, ranges = (w_in[0], CHUNKS[c][1]) if c < WO else (w_o[0], [(512 * (c - WO), 512)])
                n0 = 0
                for first, n in ranges:
                    sp.dma_start(piece(m)[:, :, n0:n0 + n],
                                 src[2 * q * P:2 * (q + 1) * P, first:first + n]
                                 .rearrange("(k p) n -> p k n", p=P)).then_inc(piece_in[m % 4], 16)
                    n0 += n
                if m == 3:
                    for dst, row in small:
                        sp.dma_start(dst, row, allow_slow_non_contiguous=True).then_inc(small_in, 16)
            sp.wait_ge(values_ok, HB + HA)
            sp.dma_start(GF, bc(g_ffn)).then_inc(gf_in, 16)
            sp.wait_ge(w_lo, 4 * (WO + 2))
            for t in range(T):
                if t >= 1:
                    sp.wait_ge(logit_ps, t)
                if t == T - 1:
                    sp.wait_ge(score_ps, SCORE["all"])
                    for h in range(2):
                        sp.dma_start(bg_raw[E * h:E * h + E, 0:2 * DE], b_gu[0]).then_inc(bg_in, 16)
                        sp.dma_start(bg_raw[E * h:E * h + E, 2 * DE:3 * DE], b_down[0]).then_inc(bg_in, 16)
                sp.dma_start(xres, x[0, rows_of(t), :]).then_inc(xres_in, 16)
                if t == T - 1:
                    for c in range(RAW):
                        sp.dma_start(chunk_dst(0, c), chunk_src(0, c)).then_inc(landed[raw_slot(0, c)], 16)
                sp.wait_ge(x1_ok, t + 1)
                sp.dma_start(out[0, rows_of(t), :], x1).then_inc(rows_out, 16)
                sp.wait_ge(h2_ok, t + 1)
                sp.dma_start(hd[rows_of(t), :], h2).then_inc(rows_out, 16)

            def load_chunk(r, i, c):
                after(sp, chunk_lo, chunk_no(r, i, c) - RAW + 1)
                sp.dma_start(chunk_dst(i, c), chunk_src(i, c)).then_inc(landed[raw_slot(i, c)], 16)

            def stream(r):
                for c in chunks_at(0):
                    if not is0(r) or c >= RAW:
                        load_chunk(r, 0, c)
                with sp.Fori(1, E) as i:
                    for c in chunks_at(i):
                        load_chunk(r, i, c)
                for c in chunks_at(E):
                    load_chunk(r, E, c)

            stream(0)
            more_rounds(sp, stream)

        @block.gpsimd
        def _(pool):
            steps = [0]

            def link(ins):
                steps[0] += 1
                ins.then_inc(pool_step, 1)
                pool.wait_ge(pool_step, steps[0])

            link(pool.memset(ident, 0.0))
            link(pool.affine_select(out=ident, in_=ident, compare_op=ALU.not_equal, fill=1.0, base=0,
                                    pattern=[[-1, P]], channel_multiplier=1))
            link(pool.tensor_copy(identb, ident))
            link(pool.memset(half, -0.5))
            link(pool.memset(causal, 0.0))
            link(pool.memset(causal[0:CHUNK, CHUNK:P], MASKED))
            link(pool.iota(iota, pattern=[[1, P]], base=0, channel_multiplier=0,
                           allow_small_or_imprecise_dtypes=True))
            link(pool.memset(ones, 1.0))
            link(pool.affine_select(out=tri, in_=ones, compare_op=ALU.is_gt, fill=0.0, base=0,
                                    pattern=[[1, P]], channel_multiplier=-1))
            link(pool.iota(tokf, pattern=[[0, 1]], base=0, channel_multiplier=1,
                           allow_small_or_imprecise_dtypes=True))
            link(pool.memset(tokg, 0.0))
            link(pool.tensor_copy(tok1, tokf.to_broadcast([P, T])))
            for t in range(T):
                link(pool.memset(tok128[:, t:t + 1], float(P * t - FAR)))
            link(pool.memset(pick, 0.0))
            for b in (0, E):
                link(pool.affine_select(out=pick, in_=pick, compare_op=ALU.not_equal, fill=1.0, base=-b,
                                        pattern=[[-1, E + 1]], channel_multiplier=1))
            link(pool.memset(zero, 0))
            pool.memset(rows, 0).then_inc(const, 1)
            pool.wait_ge(x_mean, 1)
            pool.tensor_tensor(xroot, ss[:, 4, 0:T], half[:, 0:T], ALU.pow).then_inc(x_root, 1)

            for st in PLAN:
                if st[0] == "split_w" and st[1] in POOL_SPLITS:
                    if st[1] == POOL_SPLITS[0]:
                        pool.wait_ge(w_lo, st[1])
                    split_w_lo(pool, st[1])
                elif st[0] == "norm" and st[1] in NORMED:
                    u = st[1]
                    _, view = heads_of(u)
                    pool.wait_ge(scaled, NORMED.index(u) + 1)
                    pool.tensor_tensor(view, view, gain_of(u), ALU.mult).then_inc(gained, 1)
                elif st[0] == "sums" and st[1] in NORMED:
                    u = st[1]
                    n, _ = heads_of(u)
                    k = NORMED.index(u)
                    pool.wait_ge(summed, k + 1)
                    pool.tensor_tensor(rstd[:, k % 4, 0:n], ss[:, k % 4, 0:n], half[:, 0:n],
                                       ALU.pow).then_inc(rooted, 1)
                elif st[0] == "mix_b":
                    pool.wait_ge(yss, st[1] + 1)
                    pool.tensor_tensor(rstd[:, 4, 0:HB], ss[:, 4, 0:HB], half[:, 0:HB], ALU.pow) \
                        .then_inc(yroot, 1)
                elif st[0] == "mix_norm":
                    pool.wait_ge(yroot, st[1] + 1)
                    link(pool.tensor_tensor(yB, yB, rstd[:, 4, 0:HB].unsqueeze(2)
                                            .to_broadcast([P, HB, 2 * HD]), ALU.mult))
                    pool.tensor_tensor(yB, yB, gsub.unsqueeze(1).to_broadcast([P, HB, 2 * HD]), ALU.mult) \
                        .then_inc(yb_ok, 1)
                elif st[0] == "post_mean":
                    pool.wait_ge(x1_mean, st[1] + 1)
                    pool.tensor_tensor(tss[:, 2:3], tss[:, 1:2], half[:, 0:1], ALU.pow).then_inc(x1_root, 1)

            pool.wait_ge(logit_ok, T)
            pool.memset(xg, 0.0).then_inc(xg_clear, 1)
            pool.wait_ge(chunk_lo, 1)
            split_lo(pool, 0, 0, 1)
            pool.wait_ge(xg_clear, 1)
            pool.wait_ge(rows_out, 32 * T)

            def gather(r, j):
                pool.wait_ge(idx_ok, 33 * r + j + 1)
                after(pool, xT_ps, 66 * r + 2 * j)
                for n, (a, b) in enumerate(((rows[:, 2:3], rows[:, 1:2]), (rows[:, 1:2], rows[:, 0:1]),
                                            (rows[:, 0:1], idx))):
                    after(pool, row_ok, 99 * r + 3 * j + n)
                    pool.tensor_tensor(a, b, zero, ALU.add).then_inc(row_ok, 1)
                pool.indirect_dma_start(xg, None, hd, bass.IndirectOffsetOnAxis(ap=idx, axis=0),
                                        bounds_check=SEQ - 1, oob_is_err=False).then_inc(gathered, 16)

            def scatter(r, e, col):
                pool.wait_ge(yrow_ok, E * r + e + 1)
                pool.tensor_tensor(passed[:, col:col + 1], zero, zero, ALU.add)
                pool.indirect_dma_start(out[0], bass.IndirectOffsetOnAxis(ap=rows[:, col:col + 1], axis=0),
                                        ysb, None, bounds_check=SEQ - 1, oob_is_err=False,
                                        compute_op=ALU.add) \
                    .then_inc(scattered, 16)
                pool.wait_ge(scattered, 16 * (E * r + e + 1))

            def pool_round(r):
                for j in range(3):
                    gather(r, j)
                with pool.Fori(2, E) as i:
                    scatter(r, i - 2, 2)
                    gather(r, i + 1)
                scatter(r, E - 2, 2)
                scatter(r, E - 1, 1)

            pool_round(0)
            more_rounds(pool, pool_round)

        @block.scalar
        def _(act):
            act.dma_start(gcol, g_attn[0].rearrange("(k p) -> p k", p=P), allow_slow_non_contiguous=True) \
               .then_inc(gcol_in, 16)
            for t in range(T):
                act.wait_ge(x_in[t], 16)
                act.activation(squares[:, t, :], xs[:, t, :], ACT.Square, accum_out=ss[:, 3, t:t + 1]) \
                   .then_inc(x_sum, 1)

            for st in PLAN:
                kind = st[0]
                if kind == "turn_h":
                    k, g = st[1], TURN[st]
                    act.wait_ge(turned, g + 1)
                    act.wait_ge(gcol_in, 16)
                    act.activation(HT[:, 0, k, :], tbank(g), ACT.Copy, scale=gcol[:, k:k + 1]) \
                       .then_inc(hi_ok, 1)
                elif kind == "split_w":
                    m = st[1]
                    c, q = m // 4, m % 4
                    wait_piece(act, m)
                    wait_wbuf(act, c)
                    act.activation(wbuf(c)[:, 0, 2 * q:2 * q + 2, 0:WIDTH[c]], piece(m), ACT.Copy) \
                       .then_inc(w_hi, 1)
                elif kind == "sums" and st[1] in NORMED:
                    u = st[1]
                    n, view = heads_of(u)
                    k = NORMED.index(u)
                    act.wait_ge(raw_ok, u + 1)
                    if k >= 2:
                        act.wait_ge(summed, k - 1)
                    act.activation(sq[:, k % 2, 0:n * HD].rearrange("p (h d) -> p h d", h=n), view,
                                   ACT.Square).then_inc(squared, 1)
                elif kind == "proj":
                    u = st[1]
                    act.wait_ge(projected, u + 1)
                    wait_raw(act, u)
                    n = WIDTH[ITEMS[u][0]]
                    dst = raw[:, u % 4, 0:n] if has_heads(u) else VB[:, ITEMS[u][1], :]
                    if u == 0:
                        act.wait_ge(x_root, 1)
                    act.activation(dst, ps[:, ACC + u % 2, 0:n], ACT.Copy,
                                   scale=xroot[:, ITEMS[u][1]:ITEMS[u][1] + 1]).then_inc(raw_ok, 1)
                elif kind == "split_heads":
                    u = st[1]
                    k = HEADED.index(u)
                    n, view = heads_of(u)
                    act.wait_ge(roped, k + 1)
                    wait_stack(act, u)
                    if is_key(u):
                        act.activation(stk[:, 0, 0:n, :].rearrange("p h (c d) -> p h c d", c=2),
                                       view.unsqueeze(2).to_broadcast([P, n, 2, HD]), ACT.Copy) \
                           .then_inc(heads_hi, 1)
                    else:
                        act.activation(stk[:, k % 2, 0:n, 0:HD], view, ACT.Copy).then_inc(heads_hi, 1)
                elif kind == "turn_heads":
                    u = st[1]
                    if name_of(u) == "bq":
                        act.wait_ge(score_ps, N_TOPK_SCORES)
                    if name_of(u) == "bk":
                        act.wait_ge(projected, ITEM_NO[(WO - 2, T - 1)] + 1)
                    for j in range(turns_in(st)):
                        g = TURN[st] + j
                        act.wait_ge(turned, g + 1)
                        dst = turned_heads(u, j)[1]
                        src = tbank(g)
                        src = src.rearrange("p (a b n) -> p a b n", a=2, b=2) if name_of(u) == "kvi" \
                            else src.rearrange("p (h n) -> p h n", h=4)
                        act.activation(dst, src, ACT.Copy).then_inc(turn_read[g % 2], 1)
                elif kind == "iscore":
                    v, w = SCORE[st], keys_of(st[1])
                    act.wait_ge(score_ps, v + 1)
                    if v >= 2:
                        act.wait_ge(rel_used, v - 1)
                    act.activation(rel[:, v % 2, 0:w], ps[:, S_BANK + v % 2, 0:w], ACT.Relu) \
                       .then_inc(score_read, 1)
                elif kind == "score":
                    n, v = st[1], SCORE[st]
                    t, j = n // 16, n % 16
                    w = keys_of(t)
                    act.wait_ge(max_ok, n + 1)
                    if n < 4:
                        act.wait_ge(rel_used, N_TOPK_SCORES)
                    elif 16 <= n < 20:
                        act.wait_ge(heads_lo, len(HEADED))
                    elif (n - 4) % 16 < 8 and n % 2:
                        act.wait_ge(combined, combo_no(("B", (n - 4) // 16, (n - 4) % 16 // 2)))
                    else:
                        pr = ("B", (n - 4) // 16, (n - 4) % 16 // 2) if (n - 4) % 16 < 8 \
                            else ("A", (n - 4) // 16, (n - 4) % 16 - 8)
                        act.wait_ge(turned, TURN[("turn_p", pr)] + 1)
                    if t >= 2 and j == 0:
                        act.wait_ge(y_ok, t - 1)
                    act.activation(e_of(n)[:, 0:w], ps[:, S_BANK + v % 2, 0:w], ACT.Exp,
                                   bias=nmax[:, t % 2, j:j + 1], accum_out=lsum[:, t % 2, j:j + 1]) \
                       .then_inc(score_read, 1)
                elif kind == "turn_p":
                    i, g, w = PROD[st], TURN[st], keys_of(st[1][1])
                    if HB + HA <= i < HB + HA + 2:
                        act.wait_ge(summed, len(NORMED))
                    act.wait_ge(turned, g + 1)
                    if i >= 2:
                        act.wait_ge(values_ok, i - 1)
                    act.activation(pt_of(st)[:, 0:w], tbank(g)[:, 0:w], ACT.Copy) \
                       .then_inc(turn_read[g % 2], 1)
                elif kind == "mix_b":
                    t = st[1]
                    act.wait_ge(values_ok, (HB + HA) * t + HB)
                    act.wait_ge(rl_ok, t + 1)
                    if t == 0:
                        act.wait_ge(w_lo, 4 * (WO + 2))
                    else:
                        st_y = ("turn_y", t - 1)
                        act.wait_ge(turned, through(st_y))
                    for h in range(HB):
                        act.activation(yB[:, h, :], ps[:, OB, rows_of(h)], ACT.Copy,
                                       scale=rl[:, 2 * h:2 * h + 1])
                        ins = act.activation(ps[:, OB, rows_of(h)], ps[:, OB, rows_of(h)], ACT.Square,
                                             scale=rl[:, 2 * h:2 * h + 1], accum_out=ss[:, 4, h:h + 1])
                    ins.then_inc(y_squared, 1)
                elif kind == "turn_y":
                    t = st[1]
                    for j in range(2):
                        g = TURN[st] + j
                        act.wait_ge(turned, g + 1)
                        if t >= 1:
                            act.wait_ge(acc_ps, t)
                        act.activation(yT[:, 0, 4 * j:4 * j + 4, :],
                                       tbank(g).rearrange("p (k n) -> p k n", k=4), ACT.Copy) \
                           .then_inc(hi_ok, 1)
                elif kind == "setup":
                    act.wait_ge(angles, 1)
                    act.activation(sinr[:, :, HALF:ROT], ang, ACT.Sin).then_inc(sines, 1)
                    act.activation(cosr[:, :, 0:HALF], cyc, ACT.Sin).then_inc(sines, 1)
                    act.wait_ge(lam_in, 1)
                    act.activation(lams[:, 0:2], lams[:, 2:4], ACT.Exp).then_inc(lam_exp, 1)
                elif kind == "biases":
                    act.wait_ge(bg_in, 64)
                    act.activation(bgs, bg_raw, ACT.Copy).then_inc(bg_hi, 1)
                elif kind == "post_norm" and st[1] == T - 1:
                    act.wait_ge(acc_ps, T)
                    split_hi(act, 0, 0, 0)
                elif kind == "post":
                    t = st[1]
                    act.wait_ge(x1_ok, t + 1)
                    act.activation(h2, x1, ACT.Square, accum_out=tss[:, 0:1]).then_inc(x1_sq, 1)
                elif kind == "turn_h2":
                    g = TURN[st]
                    if g % 2 == 0:
                        j = 0
                    else:
                        j = 1
                    act.wait_ge(turned, g + j + 1)
                    act.activation(h2T[:, 4 * j:4 * j + 4, :], tbank(g + j)
                                   .rearrange("p (k n) -> p k n", k=4), ACT.Copy).then_inc(turn_read[0], 1)

            split_hi(act, 0, 0, 1)
            act.wait_ge(gates_in, 1)
            act.activation(gate, gate, ACT.Exp).then_inc(gates_exp, 1)
            for c in range(2, HL):
                split_hi(act, 0, 0, c)

            def turn_x_hi(r, j):
                after(act, chunk_used, PER_ROUND * r if is0(j) else gu_done(r, j - 1))
                for b in range(2):
                    act.wait_ge(xT_ps, 66 * r + 2 * j + b + 1)
                    act.activation(xT[:, 0, 4 * b:4 * b + 4, :],
                                   ps[:, TP + b, :].rearrange("p (k n) -> p k n", k=4), ACT.Copy) \
                       .then_inc(xT_hi, 1)

            def turn_a_hi(r, e):
                after(act, chunk_used, PER_ROUND * r if is0(e) else dn_done(r, e - 1))
                for b in range(2):
                    act.wait_ge(aT_ps, 64 * r + 2 * e + b + 1)
                    act.activation(aT[:, 0, 4 * b:4 * b + 4, :],
                                   ps[:, TP + b, :].rearrange("p (k n) -> p k n", k=4), ACT.Copy) \
                       .then_inc(aT_hi, 1)

            def sigmoid(r, e):
                act.wait_ge(glu_ok, E * r + e + 1)
                act.activation(acts[:, 2, :], acts[:, 0, :], ACT.Sigmoid, scale=ALPHA).then_inc(sig_ok, 1)

            def y_rows(r, e):
                act.wait_ge(chunk_used, dn_done(r, e))
                after(act, scattered, 16 * (E * r + e))
                act.activation(mark, half[:, 0:1], ACT.Copy)
                act.activation(ysb.rearrange("p (a n) -> p a n", a=2), ps[:, DN:DN + 2, :], ACT.Copy,
                               scale=gslot[:, bass.ds(e, 1)]).then_inc(yrow_ok, 1)

            def act_body(r, i, first=False):
                for c in range(NCH - 1):
                    if not (first and c < EARLY):
                        split_hi(act, r, i, c)
                    if c == 0 and not first:
                        y_rows(r, i - 2)
                    if c == COPY_AT:
                        turn_a_hi(r, i - 1)
                turn_x_hi(r, i + 1)
                sigmoid(r, i)
                split_hi(act, r, i, NCH - 1)

            def act_round(r):
                turn_x_hi(r, 0)
                for c in range(HL if is0(r) else 0, NG):
                    split_hi(act, r, 0, c)
                for c in range(EARLY):
                    split_hi(act, r, 1, c)
                turn_x_hi(r, 1)
                sigmoid(r, 0)
                act_body(r, 1, first=True)
                act_body(r, 2)
                with act.Fori(3, E) as i:
                    act_body(r, i)
                for c in chunks_at(E):
                    split_hi(act, r, E, c)
                    if c == NG + 1:
                        y_rows(r, E - 2)
                        turn_a_hi(r, E - 1)
                y_rows(r, E - 1)

            act_round(0)
            more_rounds(act, act_round)

        @block.vector
        def _(dve):
            steps = [0]

            def link(ins):
                steps[0] += 1
                ins.then_inc(dve_step, 1)
                dve.wait_ge(dve_step, steps[0])

            dve.wait_ge(x_sum, T)
            dve.tensor_scalar(ss[:, 4, 0:T], ss[:, 3, 0:T], 1.0 / D, EPS, ALU.mult, ALU.add).then_inc(x_mean, 1)

            for st in PLAN:
                kind = st[0]
                if kind == "turn_h":
                    k, g = st[1], TURN[st]
                    dve.wait_ge(hi_ok, SPLIT[st] + 1)
                    dve.scalar_tensor_tensor(out=HT[:, 1, k, :], in0=tbank(g), scalar=gcol[:, k:k + 1],
                                             in1=HT[:, 0, k, :].bitcast(F32), op0=ALU.mult,
                                             op1=ALU.subtract).then_inc(turn_read[g % 2], 1)
                elif kind == "split_w" and st[1] not in POOL_SPLITS:
                    if st[1] == POOL_SPLITS[-1] + 1:
                        dve.wait_ge(w_lo, st[1])
                    split_w_lo(dve, st[1])
                elif kind == "sums":
                    u = st[1]
                    t = ITEMS[u][1]
                    if name_of(u) == "kvi":
                        dve.wait_ge(raw_ok, u + 1)
                        dve.tensor_scalar(iw[:, t, :], raw[:, u % 4, C_IW:C_IW + HI], (HI * HD) ** -0.5,
                                          None, ALU.mult)
                        dve.tensor_copy(VA[:, t, :], raw[:, u % 4, C_AV:C_AV + HD])
                    if u in NORMED:
                        k = NORMED.index(u)
                        n, _ = heads_of(u)
                        dve.wait_ge(squared, k + 1)
                        if k >= 4:
                            dve.wait_ge(rooted, k - 3)
                        link(dve.tensor_reduce(ss[:, k % 4, 0:n],
                                               sq[:, k % 2, 0:n * HD].rearrange("p (h d) -> p h d", h=n),
                                               AX.X, ALU.add))
                        dve.tensor_scalar(ss[:, k % 4, 0:n], ss[:, k % 4, 0:n], 1.0 / HD, EPS, ALU.mult,
                                          ALU.add).then_inc(summed, 1)
                elif kind == "norm" and st[1] in NORMED:
                    u = st[1]
                    k = NORMED.index(u)
                    n, view = heads_of(u)
                    dve.wait_ge(rooted, k + 1)
                    dve.tensor_tensor(view, view, rstd[:, k % 4, 0:n].unsqueeze(2).to_broadcast([P, n, HD]),
                                      ALU.mult).then_inc(scaled, 1)
                elif kind == "rope":
                    u = st[1]
                    t = ITEMS[u][1]
                    n, view = heads_of(u)
                    if u in NORMED:
                        dve.wait_ge(gained, NORMED.index(u) + 1)
                    else:
                        dve.wait_ge(raw_ok, u + 1)

                    def over_heads(table):
                        return table.unsqueeze(1).to_broadcast([P, n, table.shape[-1]])

                    dve.tensor_tensor(rp[:, 0, 0:n, :], view[:, :, 0:ROT], over_heads(cosr[:, t, :]), ALU.mult)
                    dve.tensor_tensor(rp[:, 1, 0:n, 0:HALF], view[:, :, HALF:ROT],
                                      over_heads(sinr[:, t, 0:HALF]), ALU.mult)
                    link(dve.tensor_tensor(rp[:, 1, 0:n, HALF:ROT], view[:, :, 0:HALF],
                                           over_heads(sinr[:, t, HALF:ROT]), ALU.mult))
                    dve.tensor_tensor(view[:, :, 0:ROT], rp[:, 0, 0:n, :], rp[:, 1, 0:n, :], ALU.add) \
                       .then_inc(roped, 1)
                elif kind == "split_heads":
                    u = st[1]
                    k = HEADED.index(u)
                    n, view = heads_of(u)
                    dve.wait_ge(heads_hi, k + 1)
                    if is_key(u):
                        for half_ in range(2):
                            cols = slice(half_ * HD, (half_ + 1) * HD)
                            ins = dve.tensor_tensor(stk[:, 1, 0:n, cols], view,
                                                    stk[:, 0, 0:n, cols].bitcast(F32), ALU.subtract)
                        ins.then_inc(heads_lo, 1)
                    else:
                        dve.tensor_tensor(stk[:, k % 2, 0:n, HD:P], view,
                                          stk[:, k % 2, 0:n, 0:HD].bitcast(F32), ALU.subtract) \
                           .then_inc(heads_lo, 1)
                elif kind == "iscore":
                    _, t, h = st
                    v, w = SCORE[st], keys_of(t)
                    dst = work[:, t - 1, 0:w]
                    dve.wait_ge(score_read, v + 1)
                    if h == 0:
                        ins = dve.tensor_scalar(dst, rel[:, v % 2, 0:w], iw[:, t, 0:1], None, ALU.mult)
                    else:
                        ins = dve.scalar_tensor_tensor(out=dst, in0=rel[:, v % 2, 0:w],
                                                       scalar=iw[:, t, h:h + 1], in1=dst, op0=ALU.mult,
                                                       op1=ALU.add)
                    ins.then_inc(rel_used, 1)
                    dve.wait_ge(rel_used, v + 1)
                    if h == HI - 1:
                        link(dve.memset(work[0:CHUNK, t - 1, w - CHUNK:w], MASKED))
                elif kind == "topk":
                    _, t, r = st
                    w = keys_of(t)
                    link(dve.max(top, work[:, t - 1, 0:w]))
                    link(dve.match_replace(work[:, t - 1, 0:w], top, work[:, t - 1, 0:w], TAKEN))
                elif kind == "mask":
                    t = st[1]
                    w = keys_of(t)
                    dve.tensor_scalar(maskA[:, t, 0:w], work[:, t - 1, 0:w], TAKEN / 2, MASKED, ALU.is_gt,
                                      ALU.mult).then_inc(mask_ok, 1)
                elif kind == "score":
                    n, v = st[1], SCORE[st]
                    t, j = n // 16, n % 16
                    dve.wait_ge(score_ps, v + 1)
                    if t >= 2 and j == 0:
                        dve.wait_ge(score_read, exp_no(16 * (t - 1) - 1))
                    dve.tensor_reduce(nmax[:, t % 2, j:j + 1], ps[:, S_BANK + v % 2, 0:keys_of(t)], AX.X,
                                      ALU.max, negate=True).then_inc(max_ok, 1)
                elif kind == "combine":
                    _, t, h = pr = st[1]
                    n, w = last_unit(pr), keys_of(t)
                    dve.wait_ge(score_read, exp_no(n))
                    rat = ratio[:, h:h + 1]
                    link(dve.reciprocal(rat, lsum[:, t % 2, 2 * h + 1:2 * h + 2]))
                    link(dve.scalar_tensor_tensor(out=rat, in0=rat, scalar=lams[:, 4:5],
                                                  in1=lsum[:, t % 2, 2 * h:2 * h + 1], op0=ALU.mult,
                                                  op1=ALU.mult))
                    dve.scalar_tensor_tensor(out=e_of(n - 1)[:, 0:w], in0=e_of(n)[:, 0:w], scalar=rat,
                                             in1=e_of(n - 1)[:, 0:w], op0=ALU.mult, op1=ALU.add) \
                       .then_inc(combined, 1)
                elif kind == "mix_b":
                    t = st[1]
                    dve.reciprocal(rl[:, 0:2 * HB], lsum[:, t % 2, 0:2 * HB]).then_inc(rl_ok, 1)
                    dve.wait_ge(y_squared, t + 1)
                    dve.tensor_scalar(ss[:, 4, 0:HB], ss[:, 4, 0:HB], 1.0 / (2 * HD), EPS, ALU.mult,
                                      ALU.add).then_inc(yss, 1)
                elif kind == "mix_a":
                    t = st[1]
                    dve.wait_ge(values_ok, (HB + HA) * (t + 1))
                    link(dve.reciprocal(rl[:, 2 * HB:], lsum[:, t % 2, 2 * HB:]))
                    dve.tensor_tensor(y[:, 0:512].rearrange("p (h d) -> p h d", h=HA),
                                      ps[:, OA, :].rearrange("p (h d) -> p h d", h=HA),
                                      rl[:, 8:16].unsqueeze(2).to_broadcast([P, HA, HD]), ALU.mult) \
                       .then_inc(y_ok, 1)
                elif kind == "turn_y":
                    for j in range(2):
                        g = TURN[st] + j
                        dve.wait_ge(hi_ok, SPLIT[st] + j + 1)
                        dve.tensor_tensor(yT[:, 1, 4 * j:4 * j + 4, :],
                                          tbank(g).rearrange("p (k n) -> p k n", k=4),
                                          yT[:, 0, 4 * j:4 * j + 4, :].bitcast(F32), ALU.subtract) \
                           .then_inc(turn_read[g % 2], 1)
                elif kind == "setup":
                    dve.wait_ge(small_in, SMALL)
                    link(dve.tensor_copy(posf, posi))
                    for j in range(HALF):
                        ins = dve.tensor_scalar(ang[:, :, j], posf, float(INV_FREQ[j]), None, ALU.mult)
                    link(ins)
                    for scale in (2.0 ** 15, 1.0):
                        link(dve.tensor_scalar(cyc, ang, 1.0 / (2 * math.pi * scale), ROUND_BY, ALU.mult, ALU.add))
                        link(dve.tensor_scalar(cyc, cyc, ROUND_BY, None, ALU.subtract))
                        for part in TWO_PI:
                            link(dve.scalar_tensor_tensor(out=ang, in0=cyc, scalar=-part * scale, in1=ang,
                                                          op0=ALU.mult, op1=ALU.add))
                    link(dve.tensor_scalar(ang, ang, PI_BELOW, -PI_BELOW, ALU.min, ALU.max))
                    link(dve.scalar_tensor_tensor(out=cyc, in0=ang, scalar=-1.0, in1=ang, op0=ALU.mult, op1=ALU.max))
                    dve.tensor_scalar(cyc, cyc, -1.0, math.pi / 2, ALU.mult, ALU.add).then_inc(angles, 1)
                    link(dve.tensor_tensor(lamv[:, 0:2, :], lamv[:, 0:2, :], lamv[:, 2:4, :], ALU.mult))
                    dve.tensor_reduce(lams[:, 2:4], lamv[:, 0:2, :], AX.X, ALU.add).then_inc(lam_in, 1)
                    link(dve.tensor_scalar(gh[:, 0:2, :], gh[:, 0:2, :], HD ** -0.5, None, ALU.mult))
                    link(dve.tensor_scalar(gsub, gsub, 1.0 - LAM_INIT, None, ALU.mult))
                    dve.wait_ge(lam_exp, 1)
                    link(dve.tensor_tensor(lams[:, 4:5], lams[:, 1:2], lams[:, 0:1], ALU.subtract))
                    link(dve.tensor_scalar(lams[:, 4:5], lams[:, 4:5], -LAM_INIT, None, ALU.add))
                    dve.wait_ge(sines, 2)
                    dve.tensor_scalar(sinr[:, :, 0:HALF], sinr[:, :, HALF:ROT], -1.0, None, ALU.mult)
                    link(dve.tensor_copy(cosr[:, :, HALF:ROT], cosr[:, :, 0:HALF]))
                elif kind == "biases":
                    dve.wait_ge(bg_hi, 1)
                    dve.tensor_tensor(bgs[E:2 * E, :], bg_raw[E:2 * E, :], bgs[E:2 * E, :].bitcast(F32),
                                      ALU.subtract).then_inc(bg_ok, 1)
                elif kind == "post":
                    t = st[1]
                    dve.wait_ge(acc_ps, t + 1)
                    dve.wait_ge(xres_in, 16 * (t + 1))
                    if t >= 1:
                        dve.wait_ge(rows_out, 32 * t)
                    dve.tensor_tensor(x1.rearrange("p (a n) -> p a n", a=2), ps[:, ACC:ACC + 2, :],
                                      xres.rearrange("p (a n) -> p a n", a=2), ALU.add).then_inc(x1_ok, 1)
                elif kind == "post_mean":
                    t = st[1]
                    dve.wait_ge(x1_sq, t + 1)
                    dve.tensor_scalar(tss[:, 1:2], tss[:, 0:1], 1.0 / D, EPS, ALU.mult, ALU.add) \
                       .then_inc(x1_mean, 1)
                elif kind == "post_norm":
                    t = st[1]
                    dve.wait_ge(x1_root, t + 1)
                    if t == 0:
                        dve.wait_ge(gf_in, 16)
                    dve.scalar_tensor_tensor(out=h2, in0=x1, scalar=tss[:, 2:3], in1=GF, op0=ALU.mult,
                                             op1=ALU.mult).then_inc(h2_ok, 1)
                elif kind == "turn_h2":
                    g = TURN[st]
                    j = 1 if g % 2 == 0 else 0
                    dve.wait_ge(turned, g + j + 1)
                    dve.tensor_copy(h2T[:, 4 * j:4 * j + 4, :], tbank(g + j)
                                    .rearrange("p (k n) -> p k n", k=4)).then_inc(turn_read[1], 1)
                elif kind == "route":
                    t = st[1]
                    if t == T - 1:
                        split_lo(dve, 0, 0, 0)
                    dve.wait_ge(logit_ps, t + 1)
                    dve.tensor_tensor(lg[:, t, :], ps[:, ACC, 0:E], brt, ALU.add).then_inc(logit_ok, 1)
                    dve.wait_ge(logit_ok, t + 1)
                    link(dve.max(top8[:, t, :], lg[:, t, :]))
                    link(dve.max_index(idx8[:, t, :], top8[:, t, :], lg[:, t, :]))

            dve.tensor_tensor(gate, top8[:, :, 0:TOPE], top8[:, :, 0:1].to_broadcast([P, T, TOPE]),
                              ALU.subtract).then_inc(gates_in, 1)
            link(dve.tensor_copy(idxf, idx8[:, :, 0:TOPE]))
            link(dve.tensor_tensor(one.rearrange("p t k e -> p (t k) e"),
                                   iota[:, 0:E].unsqueeze(1).to_broadcast([P, T * TOPE, E]),
                                   idxf.rearrange("p t k -> p (t k)").unsqueeze(2)
                                   .to_broadcast([P, T * TOPE, E]), ALU.is_equal))
            link(dve.tensor_reduce(selm, one.rearrange("p t k e -> p t e k"), AX.X, ALU.add))
            dve.tensor_copy(selb, selm).then_inc(picked, 1)
            dve.wait_ge(rank_ps, 1)
            link(dve.memset(rank, -1.0))
            link(dve.scalar_tensor_tensor(out=kef, in0=ps[:, TP + 1, 0:T * E].rearrange("p (t e) -> p t e", t=T),
                                          scalar=1.0, in1=selm, op0=ALU.add, op1=ALU.mult))
            link(dve.tensor_scalar(rank[:, :, 0:E], kef, -1.0, None, ALU.add))
            link(dve.tensor_reduce(cmax, ps[:, TP + 1, T * E:(T + 1) * E], AX.X, ALU.max))
            dve.tensor_copy(cnt, cmax).then_inc(routed, 1)

            def slots(r, j):
                after(dve, gate_ps, 33 * r + j)
                for t in range(T):
                    ins = dve.tensor_scalar(oh[:, t, :], iota, rank[:, t, bass.ds(j, 1)], None, ALU.is_equal)
                ins.then_inc(slots_ok, 1)

            def spread_gates():
                dve.wait_ge(gates_exp, 1)
                link(dve.tensor_reduce(gsum, gate, AX.X, ALU.add))
                link(dve.reciprocal(gsum, gsum))
                link(dve.tensor_tensor(gate, gate, gsum.unsqueeze(2).to_broadcast([P, T, TOPE]), ALU.mult))
                link(dve.tensor_tensor(onek.rearrange("p t k e -> p (t k) e"),
                                       one.rearrange("p t k e -> p (t k) e"),
                                       gate.rearrange("p t k -> p (t k)").unsqueeze(2)
                                       .to_broadcast([P, T * TOPE, E]), ALU.mult))
                link(dve.tensor_reduce(gden, onek.rearrange("p t k e -> p t e k"), AX.X, ALU.add))
                for n in range(3):
                    ins = dve.tensor_copy(tokg[:, :, 0:E, n], gden)
                    if n == 2:
                        ins.then_inc(gates_ok, 1)
                    else:
                        link(ins)
                        link(dve.tensor_tensor(gden, gden, tokg[:, :, 0:E, n], ALU.subtract))

            def find_rows(r, j):
                dve.wait_ge(idx_ps, 33 * r + j + 1)
                after(dve, gathered, 16 * (33 * r + j))
                after(dve, row_ok, 3 * (33 * r + j))
                dve.tensor_scalar(idx, ps[:, TP + 1, 0:1], float(FAR), None, ALU.add).then_inc(idx_ok, 1)
                if is0(r) and is0(j):
                    spread_gates()
                dve.wait_ge(gate_ps, 33 * r + j + 1)
                dve.tensor_reduce(gslot[:, bass.ds(j, 1)], ps[:, TP, 0:3], AX.X, ALU.add) \
                   .then_inc(gslot_ok, 1)
                after(dve, bias_mm, E * r + j)
                dve.tensor_copy(sel_gu, pick[:, bass.ds(j, 1)].to_broadcast([2 * E, P])).then_inc(pick_ok, 1)

            def select_down(r, i):
                after(dve, down_bias_mm, E * r + i - 1)
                dve.tensor_copy(sel_dn, pick[:, bass.ds(i - 1, 1)].to_broadcast([2 * E, P])) \
                   .then_inc(sel_ok, 1)

            slots(0, 0)

            def turn_x_lo(r, j):
                for b in range(2):
                    dve.wait_ge(xT_hi, 66 * r + 2 * j + b + 1)
                    dve.tensor_tensor(xT[:, 1, 4 * b:4 * b + 4, :],
                                      ps[:, TP + b, :].rearrange("p (k n) -> p k n", k=4),
                                      xT[:, 0, 4 * b:4 * b + 4, :].bitcast(F32), ALU.subtract) \
                       .then_inc(xT_lo, 1)

            def turn_a_lo(r, e):
                for b in range(2):
                    dve.wait_ge(aT_hi, 64 * r + 2 * e + b + 1)
                    dve.tensor_tensor(aT[:, 1, 4 * b:4 * b + 4, :],
                                      ps[:, TP + b, :].rearrange("p (k n) -> p k n", k=4),
                                      aT[:, 0, 4 * b:4 * b + 4, :].bitcast(F32), ALU.subtract) \
                       .then_inc(aT_lo, 1)

            def glu(r, e):
                dve.wait_ge(chunk_used, gu_done(r, e))
                after(dve, act_ok, E * r + e)
                dve.tensor_scalar(acts[:, 0, :].rearrange("p (a n) -> p a n", a=2), ps[:, GU:GU + 2, :],
                                  LIMIT, None, ALU.min).then_inc(glu_ok, 1)

            def lin(r, e):
                dve.tensor_scalar(acts[:, 1, :].rearrange("p (a n) -> p a n", a=2), ps[:, GU + 2:GU + 4, :],
                                  LIMIT, -LIMIT, ALU.min, ALU.max).then_inc(lin_ok, 1)
                dve.wait_ge(lin_ok, E * r + e + 1)
                dve.scalar_tensor_tensor(out=acts[:, 1, :], in0=acts[:, 1, :], scalar=1.0, in1=acts[:, 0, :],
                                         op0=ALU.add, op1=ALU.mult).then_inc(prod_ok, 1)

            def activate(r, e):
                dve.wait_ge(prod_ok, E * r + e + 1)
                dve.wait_ge(sig_ok, E * r + e + 1)
                after(dve, aT_ps, 64 * r + 2 * e)
                dve.tensor_tensor(acts[:, 3, :], acts[:, 1, :], acts[:, 2, :], ALU.mult).then_inc(act_ok, 1)

            def start_of(r):
                find_rows(r, 0)
                slots(r, 1)

            def dve_round(r):
                if not is0(r):
                    dve.tensor_scalar(iota, iota, float(P), None, ALU.add).then_inc(round_step, 1)
                    dve.wait_ge(round_step, r)
                    slots(r, 0)
                start_of(r)
                for c in range(NG):
                    if is0(r) and c == 2:
                        dve.wait_ge(chunk_lo, 2)
                    if not is0(r) or c >= 2:
                        split_lo(dve, r, 0, c)
                    if c == (2 if is0(r) else 0):
                        turn_x_lo(r, 0)
                    if c == HL:
                        find_rows(r, 1)
                for c in range(EARLY):
                    split_lo(dve, r, 1, c)
                glu(r, 0)
                turn_x_lo(r, 1)
                lin(r, 0)
                activate(r, 0)
                dve_body(r, 1, first=True)
                with dve.Fori(2, E) as i:
                    dve_body(r, i)
                select_down(r, E)
                for c in chunks_at(E):
                    split_lo(dve, r, E, c)
                    if c == NG + 1:
                        turn_a_lo(r, E - 1)

            def dve_body(r, i, first=False):
                for c in range(NCH - 1):
                    if not (first and c < EARLY):
                        split_lo(dve, r, i, c)
                    if c == 0:
                        slots(r, i + 1)
                        select_down(r, i)
                    if c == COPY_AT:
                        turn_a_lo(r, i - 1)
                    if c == HL + 1:
                        find_rows(r, i + 1)
                glu(r, i)
                turn_x_lo(r, i + 1)
                lin(r, i)
                split_lo(dve, r, i, NCH - 1)
                activate(r, i)

            dve_round(0)
            more_rounds(dve, dve_round)

        @block.tensor
        def _(pe):
            def three(dst, a, b, k_first, k_last):
                pe.matmul(dst, a[0], b[0], start=k_first, stop=False)
                pe.matmul(dst, a[0], b[1], start=False, stop=False)
                return pe.matmul(dst, a[1], b[0], start=False, stop=k_last)

            def turn(g, sources):
                wait_bank(pe, g)
                for j, s_ in enumerate(sources):
                    ins = pe.transpose(tbank(g)[:, j * P:(j + 1) * P], s_, ident)
                ins.then_inc(turned, 1)

            pe.wait_ge(const, 1)
            for t in range(T):
                pe.wait_ge(x_in[t], 16)
            for st in PLAN:
                kind = st[0]
                if kind == "turn_h":
                    turn(TURN[st], [xs[:, t, st[1] * P:(st[1] + 1) * P] for t in range(T)])
                elif kind == "proj":
                    u = st[1]
                    c, t = ITEMS[u]
                    if u == 0:
                        wait_turns(pe, KD)
                    if u >= 2:
                        pe.wait_ge(raw_ok, u - 1)
                    dst = ps[:, ACC + u % 2, 0:WIDTH[c]]
                    for k in range(KD):
                        if k % 2 == 0:
                            pe.wait_ge(w_lo, 4 * c + k // 2 + 1)
                        ins = three(dst, [HT[:, a, k, rows_of(t)] for a in range(2)],
                                    [wbuf(c)[:, b, k, 0:WIDTH[c]] for b in range(2)], k == 0, k == KD - 1)
                    ins.then_inc(projected, 1)
                elif kind == "turn_heads":
                    u = st[1]
                    pe.wait_ge(heads_lo, HEADED.index(u) + 1)
                    for j in range(turns_in(st)):
                        turn(TURN[st] + j, [s_.bitcast(F32) for s_ in turned_heads(u, j)[0]])
                elif kind == "iscore":
                    _, t, h = st
                    v, w = SCORE[st], keys_of(t)
                    if v == 0:
                        wait_turns(pe, through(("turn_heads", ITEM_NO[(1, T - 1)])))
                    if v >= 2:
                        pe.wait_ge(score_read, v - 1)
                    dst = ps[:, S_BANK + v % 2, 0:w]
                    pe.matmul(dst, IQ[:, h, rows_of(t)], KAI[:, 0, 0, 0:w], start=True, stop=False)
                    pe.matmul(dst, IQ[:, h, rows_of(t)], KAI[:, 0, 1, 0:w], start=False, stop=True) \
                      .then_inc(score_ps, 1)
                elif kind == "score":
                    n, v = st[1], SCORE[st]
                    t, j = n // 16, n % 16
                    w = keys_of(t)
                    if j == 0:
                        wait_turns(pe, through(("turn_heads", ITEM_NO[(WO - 1, t)])))
                    pe.wait_ge(score_read, v - 1)
                    dst = ps[:, S_BANK + v % 2, 0:w]
                    if j < 8:
                        q, keys = QB[:, j, rows_of(t)], [KB[:, a, j, 0:w] for a in range(2)]
                    else:
                        q, keys = QA[:, j - 8, rows_of(t)], [KAI[:, 1, a, 0:w] for a in range(2)]
                    pe.matmul(dst, q, keys[0], start=True, stop=False)
                    if j < 8 or t == 0:
                        pe.matmul(dst[:, w - P:w], identb, causal, start=False, stop=False)
                    else:
                        if j == 8:
                            pe.wait_ge(mask_ok, t)
                        pe.matmul(dst, identb, maskA[:, t, 0:w], start=False, stop=False)
                    pe.matmul(dst, q, keys[1], start=False, stop=True).then_inc(score_ps, 1)
                elif kind == "turn_p":
                    pr = st[1]
                    if pr[0] == "B":
                        pe.wait_ge(combined, combo_no(pr))
                    else:
                        pe.wait_ge(score_read, exp_no(last_unit(pr)))
                    turn(TURN[st], [e_in(pr)[:, rows_of(b)] for b in range(pr[1] + 1)])
                elif kind == "values":
                    pr = st[1]
                    which, t, h = pr
                    i, g = PROD[("turn_p", pr)], TURN[("turn_p", pr)]
                    pe.wait_ge(turn_read[g % 2], g // 2 + 1)
                    if which == "B" and h == 0 and t >= 1:
                        pe.wait_ge(yss, t)
                    if which == "A" and h == 0 and t >= 1:
                        pe.wait_ge(y_ok, t)
                    for b in range(t + 1):
                        if which == "B":
                            dst, val = ps[:, OB, h * P:(h + 1) * P], VB[:, b, h * P:(h + 1) * P]
                        else:
                            dst, val = ps[:, OA, h * HD:(h + 1) * HD], VA[:, b, :]
                        ins = pe.matmul(dst, pt_of(("turn_p", pr))[:, rows_of(b)], val, start=(b == 0), stop=(b == t))
                    ins.then_inc(values_ok, 1)
                elif kind == "turn_y":
                    t = st[1]
                    pe.wait_ge(y_ok, t + 1)
                    pe.wait_ge(yb_ok, t + 1)
                    for j in range(2):
                        turn(TURN[st] + j, [y[:, (4 * j + k) * P:(4 * j + k + 1) * P] for k in range(4)])
                elif kind == "out_proj":
                    _, t, k = st
                    if k == 0:
                        wait_turns(pe, through(("turn_y", t)))
                        pe.wait_ge(w_lo, 4 * (WO + 2))
                        if t >= 1:
                            pe.wait_ge(logit_ok, t)
                    for h in range(2):
                        ins = three(ps[:, ACC + h, :], [yT[:, a, k, :] for a in range(2)],
                                    [wbuf(WO + h)[:, b, k, :] for b in range(2)], k == 0, k == KD - 1)
                    if k == KD - 1:
                        ins.then_inc(acc_ps, 1)
                elif kind == "turn_h2":
                    t = st[1]
                    pe.wait_ge(h2_ok, t + 1)
                    for j in range(2):
                        turn(TURN[st] + j, [h2[:, (4 * j + k) * P:(4 * j + k + 1) * P] for k in range(4)])
                elif kind == "route":
                    t = st[1]
                    wait_turns(pe, through(("turn_h2", t)))
                    for k in range(KD):
                        ins = pe.matmul(ps[:, ACC, 0:E], h2T[:, k, :], wrt[:, k, :], start=(k == 0),
                                        stop=(k == KD - 1))
                    ins.then_inc(logit_ps, 1)

            pe.wait_ge(picked, 1)
            for t in range(T):
                dst = ps[:, TP + 1, t * E:(t + 1) * E]
                for b in range(t):
                    pe.matmul(dst, ones, selb[:, b, :], start=(b == 0), stop=False)
                pe.matmul(dst, tri, selb[:, t, :], start=(t == 0), stop=True)
            for b in range(T):
                ins = pe.matmul(ps[:, TP + 1, T * E:(T + 1) * E], ones, selb[:, b, :], start=(b == 0),
                                stop=(b == T - 1))
            ins.then_inc(rank_ps, 1)

            def find(r, j):
                pe.wait_ge(slots_ok, 33 * r + j + 1)
                if is0(r) and is0(j):
                    pe.wait_ge(routed, 1)
                else:
                    pe.wait_ge(gslot_ok, 33 * r + j)
                dst = ps[:, TP + 1, 0:1]
                for t in range(T):
                    pe.matmul(dst, oh[:, t, :], tok1[:, t:t + 1], start=(t == 0), stop=False)
                    ins = pe.matmul(dst, oh[:, t, :], tok128[:, t:t + 1], start=False,
                                    stop=(t == T - 1))
                ins.then_inc(idx_ps, 1)
                if is0(r) and is0(j):
                    pe.wait_ge(gates_ok, 1)
                for t in range(T):
                    ins = pe.matmul(ps[:, TP, 0:3], oh[:, t, :], tokg[:, t, bass.ds(j, 1), :], start=(t == 0),
                                    stop=(t == T - 1))
                ins.then_inc(gate_ps, 1)

            def turn_x(r, j):
                pe.wait_ge(gathered, 16 * (33 * r + j + 1))
                for b in range(2):
                    for k in range(4):
                        ins = pe.transpose(ps[:, TP + b, k * P:(k + 1) * P],
                                           xg[:, (4 * b + k) * P:(4 * b + k + 1) * P], ident)
                    ins.then_inc(xT_ps, 1)

            def turn_a(r, e):
                pe.wait_ge(act_ok, E * r + e + 1)
                pe.wait_ge(xT_lo, 66 * r + 2 * e + 4)
                for b in range(2):
                    for k in range(4):
                        ins = pe.transpose(ps[:, TP + b, k * P:(k + 1) * P],
                                           acts[:, 3, (4 * b + k) * P:(4 * b + k + 1) * P], ident)
                    ins.then_inc(aT_ps, 1)

            def chunk_products(r, i, c, a, banks):
                pe.wait_ge(chunk_lo, chunk_no(r, i, c) + 1)
                nj = len(a[0])
                w = whl[:, c % HL].rearrange("p s (j n) -> p s j n", j=nj)
                last = c in (NG - 1, NCH - 1)
                for j in range(nj):
                    for n, (x_, b) in enumerate(((0, 0), (0, 1), (1, 0))):
                        for q, bank in enumerate(banks):
                            ins = pe.matmul(bank, a[x_][j], w[:, b, j, 512 * q:512 * q + 512],
                                            start=False, stop=last and j == nj - 1 and n == 2)
                ins.then_inc(chunk_used, 1)

            def gate_up(r, i):
                pe.wait_ge(pick_ok, 33 * r + i + 1)
                after(pe, lin_ok, E * r + i)
                banks = [ps[:, GU + q, :] for q in range(4)]
                for q, bank in enumerate(banks):
                    ins = pe.matmul(bank, sel_gu, bgs[:, 512 * q:512 * q + 512], start=True, stop=False)
                ins.then_inc(bias_mm, 1)
                pe.wait_ge(xT_lo, 66 * r + 2 * i + 2)
                for c in range(NG):
                    chunk_products(r, i, c, [[xT[:, a, c, :]] for a in range(2)], banks)
                    if c == TURN_AT and not is0(i):
                        turn_a(r, i - 1)
                    if c == FIND_AT:
                        if is0(i):
                            find(r, 1)
                        else:
                            find_next(r, i + 1)

            def down(r, i):
                banks = [ps[:, DN + q, :] for q in range(2)]
                pe.wait_ge(aT_lo, 64 * r + 2 * i)
                for c in range(NG, NCH):
                    k = 2 * (c - NG)
                    if c == NG:
                        pe.wait_ge(sel_ok, E * r + i)
                        after(pe, yrow_ok, E * r + i - 1)
                        for q, bank in enumerate(banks):
                            ins = pe.matmul(bank, sel_dn, bgs[:, 2 * DE + 512 * q:2 * DE + 512 * q + 512],
                                            start=True, stop=False)
                        ins.then_inc(down_bias_mm, 1)
                    chunk_products(r, i, c, [[aT[:, a, k + j, :] for j in range(2)] for a in range(2)], banks)

            def find_next(r, j):
                after(pe, aT_lo, 64 * r + 2 * (j - 1) if not is0(j - 1) else 64 * r)
                find(r, j)

            def pe_body(r, i):
                gate_up(r, i)
                pe.wait_ge(gslot_ok, 33 * r + i + 2)
                turn_x(r, i + 1)
                down(r, i)

            def pe_round(r):
                if not is0(r):
                    pe.wait_ge(aT_lo, 64 * r)
                find(r, 0)
                if is0(r):
                    pe.wait_ge(bg_ok, 1)
                pe.wait_ge(gslot_ok, 33 * r + 1)
                turn_x(r, 0)
                pe.wait_ge(xT_lo, 66 * r + 2)
                gate_up(r, 0)
                pe.wait_ge(gslot_ok, 33 * r + 2)
                turn_x(r, 1)
                pe_body(r, 1)
                with pe.Fori(2, E) as i:
                    pe_body(r, i)
                turn_a(r, E - 1)
                down(r, E)

            pe_round(0)
            more_rounds(pe, pe_round)


_INS = ['x', 'positions', 'g_attn', 'w_in', 'g_qa', 'g_ka', 'g_idx_k', 'lambda_q1', 'lambda_k1',
        'lambda_q2', 'lambda_k2', 'g_qb', 'g_kb', 'g_subln', 'w_o', 'g_ffn', 'w_router', 'b_router',
        'w_gu', 'b_gu', 'w_down', 'b_down']
_OUTS = [((1, SEQ, D), 'float32')]


def kernel(**inputs):
    import concourse.bacc as _bacc
    from concourse.bass_utils import run_bass_kernel_spmd as _run

    nc = _bacc.Bacc("TRN2", target_bir_lowering=False, num_devices=1)
    arrays, args = {}, []
    for name in _INS:
        a = np.ascontiguousarray(inputs[name])
        arrays[f"in_{name}_dram"] = a
        args.append(nc.dram_tensor(f"in_{name}_dram", a.shape, mybir.dt.from_np(a.dtype), kind="ExternalInput").ap())
    for i, (shape, dtype) in enumerate(_OUTS):
        dt = mybir.dt.from_np(np.dtype(dtype))
        args.append(nc.dram_tensor(f"out_{i}_dram", shape, dt, kind="ExternalOutput").ap())
    build(nc, *args)
    r = _run(nc, [arrays], core_ids=[0])
    return r.results[0]["out_0_dram"]
```
